# Optimizing a Trainium2 kernel written in Bass

```python
import math
import jax, jax.numpy as jnp
from jax import lax
import numpy as np

D_MODEL = 1024
BATCH = 1
SEQ = 512
DEPTH = 2

N_MIXERS = 2
D_FF = 4 * D_MODEL
NORM_EPS = 1e-6
GLA_HEADS = 4
GLA_DK = D_MODEL // 2 // GLA_HEADS
GLA_DV = D_MODEL // GLA_HEADS
GLA_GATE_RANK = 16
GLA_TAU = 16.0
GLA_CHUNK = 64
GLA_IN = 2 * GLA_HEADS * GLA_DK + 2 * D_MODEL + GLA_GATE_RANK
DIFF_HEADS = 8
DIFF_DH = D_MODEL // DIFF_HEADS // 2
DIFF_DV = 2 * DIFF_DH
DIFF_IN = 3 * D_MODEL
ROPE_THETA = 500000.0
ROPE_DIM = DIFF_DH // 4
Q_BLOCK = 128
N_GLA = (DEPTH + 1) // 2
N_DIFF = DEPTH // 2


def rmsnorm(x, g):
    xf = x.astype(jnp.float32)
    y = xf * lax.rsqrt(jnp.mean(xf * xf, axis=-1, keepdims=True) + NORM_EPS)
    return (y * g.astype(jnp.float32)).astype(x.dtype)

def rope_partial(x, cos, sin):
    half = ROPE_DIM // 2
    cos = cos.astype(x.dtype)
    sin = sin.astype(x.dtype)
    x1 = x[..., :half]
    x2 = x[..., half:ROPE_DIM]
    rest = x[..., ROPE_DIM:]
    return jnp.concatenate([x1 * cos - x2 * sin, x2 * cos + x1 * sin, rest], axis=-1)

def gla_mixer(h, w_in, w_a2, b_a, b_r, norm_g, w_o):
    B, T, _ = h.shape
    H, dk, dv, C = GLA_HEADS, GLA_DK, GLA_DV, GLA_CHUNK
    n = T // C
    hk = H * dk
    f32 = jnp.float32
    q, k, v, r, a_lr = jnp.split(h @ w_in, [hk, 2 * hk, 2 * hk + D_MODEL, 2 * hk + 2 * D_MODEL], axis=-1)
    log_a = jax.nn.log_sigmoid((a_lr @ w_a2 + b_a).astype(f32)) / GLA_TAU

    def chunks(t, d):
        return t.reshape(B, n, C, H, d)

    q = chunks(q.astype(f32), dk) * (dk ** -0.5)
    k = chunks(k.astype(f32), dk)
    v = chunks(v.astype(f32), dv)
    b = jnp.cumsum(chunks(log_a, dk), axis=2)
    b_last = b[:, :, -1:]
    q_dec = q * jnp.exp(b)
    k_intra = k * jnp.exp(-b)
    k_state = k * jnp.exp(b_last - b)

    causal = jnp.tril(jnp.ones((C, C), dtype=bool))
    scores = jnp.einsum('bnchk,bnshk->bnhcs', q_dec, k_intra)
    scores = jnp.where(causal, scores, 0.0)
    o_intra = jnp.einsum('bnhcs,bnshv->bnchv', scores, v)

    def step(state, inp):
        q_c, k_c, v_c, decay = inp
        o_c = jnp.einsum('bchk,bhkv->bchv', q_c, state)
        state = state * jnp.exp(decay)[..., None] + jnp.einsum('bchk,bchv->bhkv', k_c, v_c)
        return state, o_c

    xs = (jnp.moveaxis(q_dec, 1, 0), jnp.moveaxis(k_state, 1, 0),
          jnp.moveaxis(v, 1, 0), jnp.moveaxis(b_last[:, :, 0], 1, 0))
    s0 = jnp.zeros((B, H, dk, dv), f32)
    _, o_inter = lax.scan(step, s0, xs)
    o = o_intra + jnp.moveaxis(o_inter, 0, 1)
    o = rmsnorm(o, norm_g).reshape(B, T, D_MODEL)
    o = o * jax.nn.silu((r + b_r).astype(f32))
    return o.astype(h.dtype) @ w_o

def diff_mixer(h, cos, sin, w_in, lam_vecs, subln_g, w_o, lambda_init):
    B, T, _ = h.shape
    H, dh, dv = DIFF_HEADS, DIFF_DH, DIFF_DV
    f32 = jnp.float32
    q, k, v = jnp.split(h @ w_in, 3, axis=-1)
    q = rope_partial(q.reshape(B, T, H, 2, dh), cos, sin) * (dh ** -0.5)
    k = rope_partial(k.reshape(B, T, H, 2, dh), cos, sin)
    q = q.transpose(0, 2, 3, 1, 4)
    k = k.transpose(0, 2, 3, 1, 4)
    v = v.reshape(B, T, H, dv).transpose(0, 2, 1, 3)
    lf = lam_vecs.astype(f32)
    lam = jnp.exp(jnp.sum(lf[0] * lf[1])) - jnp.exp(jnp.sum(lf[2] * lf[3])) + lambda_init
    outs = []
    for i in range(T // Q_BLOCK):
        L = (i + 1) * Q_BLOCK
        qb = q[:, :, :, i * Q_BLOCK:L]
        s = jnp.einsum('bhiqd,bhikd->bhiqk', qb, k[:, :, :, :L]).astype(f32)
        q_idx = i * Q_BLOCK + jnp.arange(Q_BLOCK)
        mask = jnp.arange(L)[None, :] <= q_idx[:, None]
        p = jax.nn.softmax(jnp.where(mask, s, -jnp.inf), axis=-1)
        a = p[:, :, 0] - lam * p[:, :, 1]
        outs.append(jnp.einsum('bhqk,bhkv->bhqv', a.astype(v.dtype), v[:, :, :L]))
    o = jnp.concatenate(outs, axis=2)
    o = rmsnorm(o, subln_g) * (1.0 - lambda_init)
    o = o.transpose(0, 2, 1, 3).reshape(B, T, D_MODEL)
    return o @ w_o

def first_inputs(seed: int = 0) -> dict:
    key = jax.random.key(seed)
    ks = jax.random.split(key, 24)
    D = D_MODEL
    nrm = jax.random.normal
    x = nrm(ks[0], (BATCH, SEQ, D), jnp.float32)
    c = nrm(ks[1], (BATCH, D), jnp.float32)
    offsets = jax.random.randint(ks[2], (BATCH, 1), 0, 4096, dtype=jnp.int32)
    positions = (offsets + jnp.arange(SEQ, dtype=jnp.int32)[None, :]).astype(jnp.int32)
    return {
        "x": x,
        "c": c,
        "positions": positions,
        "ada_w": nrm(ks[3], (DEPTH, D, 6 * D), jnp.float32) * (0.5 * D ** -0.5),
        "ada_b": nrm(ks[4], (DEPTH, 6 * D), jnp.float32) * 0.02,
        "norm_g": 1.0 + 0.05 * nrm(ks[5], (DEPTH, 2, D), jnp.float32),
        "mlp_w1": nrm(ks[6], (DEPTH, D, D_FF), jnp.float32) * D ** -0.5,
        "mlp_w2": nrm(ks[7], (DEPTH, D_FF, D), jnp.float32) * D_FF ** -0.5,
        "gla_w_in": nrm(ks[8], (N_GLA, D, GLA_IN), jnp.float32) * D ** -0.5,
        "gla_w_a2": nrm(ks[9], (N_GLA, GLA_GATE_RANK, GLA_HEADS * GLA_DK), jnp.float32) * GLA_GATE_RANK ** -0.5,
        "gla_b_a": 0.5 + 0.1 * nrm(ks[10], (N_GLA, GLA_HEADS * GLA_DK), jnp.float32),
        "gla_b_r": 0.02 * nrm(ks[11], (N_GLA, D), jnp.float32),
        "gla_norm_g": 1.0 + 0.05 * nrm(ks[12], (N_GLA, GLA_DV), jnp.float32),
        "gla_w_o": nrm(ks[13], (N_GLA, D, D), jnp.float32) * D ** -0.5,
        "diff_w_in": nrm(ks[14], (N_DIFF, D, DIFF_IN), jnp.float32) * D ** -0.5,
        "diff_lambda": 0.1 * nrm(ks[15], (N_DIFF, 4, DIFF_DH), jnp.float32),
        "diff_subln_g": 1.0 + 0.05 * nrm(ks[16], (N_DIFF, DIFF_DV), jnp.float32),
        "diff_w_o": nrm(ks[17], (N_DIFF, D, D), jnp.float32) * D ** -0.5,
        "final_g": 1.0 + 0.05 * nrm(ks[18], (D,), jnp.float32),
    }

def first_block(x, c, positions, ada_w, ada_b, norm_g, mlp_w1, mlp_w2,
              gla_w_in, gla_w_a2, gla_b_a, gla_b_r, gla_norm_g, gla_w_o,
              diff_w_in, diff_lambda, diff_subln_g, diff_w_o, final_g):
    f32 = jnp.float32
    inv_freq = ROPE_THETA ** (-jnp.arange(0, ROPE_DIM, 2, dtype=f32) / ROPE_DIM)
    ang = positions.astype(f32)[..., None] * inv_freq
    cos = jnp.cos(ang)[:, :, None, None, :]
    sin = jnp.sin(ang)[:, :, None, None, :]
    c_act = jax.nn.silu(c)
    for i in range(DEPTH):
        mod = c_act @ ada_w[i] + ada_b[i]
        shift_t, scale_t, gate_t, shift_c, scale_c, gate_c = [
            m[:, None, :] for m in jnp.split(mod, 6, axis=-1)]
        h = rmsnorm(x, norm_g[i, 0]) * (1.0 + scale_t) + shift_t
        j = i // N_MIXERS
        if i % N_MIXERS == 0:
            y = gla_mixer(h, gla_w_in[j], gla_w_a2[j], gla_b_a[j], gla_b_r[j],
                          gla_norm_g[j], gla_w_o[j])
        else:
            lambda_init = 0.8 - 0.6 * math.exp(-0.3 * i)
            y = diff_mixer(h, cos, sin, diff_w_in[j], diff_lambda[j], diff_subln_g[j],
                           diff_w_o[j], lambda_init)
        x = x + gate_t * y
        h = rmsnorm(x, norm_g[i, 1]) * (1.0 + scale_c) + shift_c
        y = jnp.square(jax.nn.relu(h @ mlp_w1[i])) @ mlp_w2[i]
        x = x + gate_c * y
    return rmsnorm(x, final_g)


DEPTH_2 = 1

CHUNK = 64

A_HEADS = 4
A_HEAD_DIM = 128
A_WIDTH = A_HEADS * A_HEAD_DIM
A_KV_RANK = 128
IDX_HEADS = 8
IDX_DIM = 64
TOPK_MAX = 256

B_HEADS = 4
B_KEY_DIM = 128
B_VAL_DIM = 128
B_WIDTH = B_HEADS * B_VAL_DIM
B_FORGET = B_HEADS * B_KEY_DIM

D_MIX = A_WIDTH + B_WIDTH

REL_BUCKETS = 32
REL_MAX_DIST = 256

DEEPNORM_ALPHA = (2.0 * DEPTH_2) ** 0.25
DEEPNORM_BETA = (8.0 * DEPTH_2) ** -0.25
LN_EPS = 1e-5
RMS_EPS = 1e-6

_SPLITS = (
    ('a_q', A_WIDTH),
    ('a_ckv', A_KV_RANK),
    ('a_iq', IDX_HEADS * IDX_DIM),
    ('a_ik', IDX_DIM),
    ('a_iw', IDX_HEADS),
    ('a_gate', A_WIDTH),
    ('b_q', B_FORGET),
    ('b_f', B_FORGET),
    ('b_i', B_WIDTH),
    ('b_gate', B_WIDTH),
)
D_IN_PROJ = int(sum(n for _, n in _SPLITS))
SPLIT_POINTS = tuple(int(v) for v in np.cumsum([n for _, n in _SPLITS])[:-1])


def _rms_norm(x, g):
    xf = x.astype(jnp.float32)
    y = xf * lax.rsqrt(jnp.mean(xf * xf, axis=-1, keepdims=True) + RMS_EPS)
    return (y * g.astype(jnp.float32)).astype(x.dtype)

def _layer_norm(x, g, b):
    xf = x.astype(jnp.float32)
    mu = jnp.mean(xf, axis=-1, keepdims=True)
    var = jnp.mean(jnp.square(xf - mu), axis=-1, keepdims=True)
    y = (xf - mu) * lax.rsqrt(var + LN_EPS) * g.astype(jnp.float32) + b.astype(jnp.float32)
    return y.astype(x.dtype)

def _t5_bucket(rel):
    nb = REL_BUCKETS // 2
    max_exact = nb // 2
    ret = jnp.where(rel > 0, nb, 0).astype(jnp.int32)
    n = jnp.abs(rel)
    nf = jnp.maximum(n, 1).astype(jnp.float32)
    large = max_exact + (jnp.log(nf / max_exact) / math.log(REL_MAX_DIST / max_exact)
                         * (nb - max_exact)).astype(jnp.int32)
    large = jnp.minimum(large, nb - 1)
    return ret + jnp.where(n < max_exact, n, large)

def _dsa_mixer(q, c, iq, ik, iw, w_uk, rel_bias):
    bsz, seq = q.shape[0], q.shape[1]
    k_sel = min(TOPK_MAX, seq // 4)
    n_blk = seq // Q_BLOCK
    q_lat = jnp.einsum('bshd,hdr->bshr', q, w_uk)
    scale = A_HEAD_DIM ** -0.5
    idx_scale = IDX_DIM ** -0.5
    w_scale = IDX_HEADS ** -0.5
    pos = jnp.arange(seq, dtype=jnp.int32)
    key_chunk = pos // CHUNK

    def blockify(t):
        return jnp.moveaxis(t.reshape(bsz, n_blk, Q_BLOCK, *t.shape[2:]), 1, 0)

    xs = (blockify(q_lat), blockify(iq), blockify(iw), pos.reshape(n_blk, Q_BLOCK))

    def one_block(args):
        ql, iqb, iwb, qpos = args
        q_chunk = qpos // CHUNK
        admissible = key_chunk[None, :] <= q_chunk[:, None]
        dots = jnp.einsum('bqhd,bsd->bqhs', iqb, ik) * idx_scale
        score = jnp.einsum('bqh,bqhs->bqs', iwb * w_scale, jax.nn.relu(dots))
        score = jnp.where(admissible[None], score.astype(jnp.float32), -jnp.inf)
        _, sel = lax.top_k(score, k_sel)
        valid = (sel // CHUNK) <= q_chunk[None, :, None]
        c_sel = jax.vmap(lambda cb, ib: cb[ib])(c, sel)
        bias = rel_bias[_t5_bucket(sel - qpos[None, :, None])]
        logits = (jnp.einsum('bqhr,bqkr->bqhk', ql, c_sel).astype(jnp.float32) * scale
                  + jnp.swapaxes(bias, -1, -2).astype(jnp.float32))
        logits = jnp.where(valid[:, :, None, :], logits, -jnp.inf)
        p = jax.nn.softmax(logits, axis=-1).astype(c.dtype)
        return jnp.einsum('bqhk,bqkr->bqhr', p, c_sel)

    o = lax.map(one_block, xs)
    return jnp.moveaxis(o, 0, 1).reshape(bsz, seq, A_HEADS, A_KV_RANK)

def _hgrn2_mixer(q, f_raw, v, lb):
    bsz, seq = q.shape[0], q.shape[1]
    n_chunk = seq // CHUNK
    q = jax.nn.silu(q.astype(jnp.float32))
    lbh = lb.reshape(B_HEADS, B_KEY_DIM).astype(jnp.float32)
    f = lbh + (1.0 - lbh) * jax.nn.sigmoid(f_raw.astype(jnp.float32))
    k = 1.0 - f
    log_f = jnp.log(f)

    def chunkify(t):
        return jnp.transpose(t.reshape(bsz, n_chunk, CHUNK, B_HEADS, t.shape[-1]), (1, 0, 3, 2, 4))

    qc, kc, vc = chunkify(q), chunkify(k), chunkify(v.astype(jnp.float32))
    bc = jnp.cumsum(chunkify(log_f), axis=3)
    causal = jnp.tril(jnp.ones((CHUNK, CHUNK), dtype=bool))

    def step(state, inp):
        qn, kn, vn, bn = inp
        diff = bn[:, :, :, None, :] - bn[:, :, None, :, :]
        decay = jnp.exp(jnp.where(causal[:, :, None], diff, -jnp.inf))
        scores = jnp.einsum('bhtk,bhsk,bhtsk->bhts', qn, kn, decay)
        o = (jnp.einsum('bhts,bhsv->bhtv', scores, vn)
             + jnp.einsum('bhtk,bhkv->bhtv', qn * jnp.exp(bn), state))
        b_last = bn[:, :, -1:, :]
        state = (jnp.exp(b_last[:, :, 0, :])[..., None] * state
                 + jnp.einsum('bhsk,bhsv->bhkv', kn * jnp.exp(b_last - bn), vn))
        return state, o

    s0 = jnp.zeros((bsz, B_HEADS, B_KEY_DIM, B_VAL_DIM), jnp.float32)
    _, o = lax.scan(step, s0, (qc, kc, vc, bc))
    return jnp.transpose(o, (1, 0, 3, 2, 4)).reshape(bsz, seq, B_HEADS, B_VAL_DIM)

def second_inputs(seed: int = 0) -> dict:
    key = jax.random.key(seed)
    ks = jax.random.split(key, 12)
    x = jax.random.normal(ks[0], (BATCH, SEQ, D_MODEL), jnp.float32)
    col_scale = jnp.concatenate([
        jnp.full((n,), DEEPNORM_BETA if name == 'b_i' else 1.0, jnp.float32) for name, n in _SPLITS])
    w_in = jax.random.normal(ks[1], (DEPTH_2, D_MODEL, D_IN_PROJ), jnp.float32) * (D_MODEL ** -0.5) * col_scale
    w_uk = jax.random.normal(ks[2], (DEPTH_2, A_HEADS, A_HEAD_DIM, A_KV_RANK), jnp.float32) * (A_HEAD_DIM ** -0.5)
    w_uv = (jax.random.normal(ks[3], (DEPTH_2, A_HEADS, A_KV_RANK, A_HEAD_DIM), jnp.float32)
            * (A_KV_RANK ** -0.5) * DEEPNORM_BETA)
    kv_norm_g = 1.0 + 0.05 * jax.random.normal(ks[4], (DEPTH_2, A_KV_RANK), jnp.float32)
    rel_bias = 0.2 * jax.random.normal(ks[5], (REL_BUCKETS, A_HEADS), jnp.float32)
    lb_logits = 0.5 * jax.random.normal(ks[6], (DEPTH_2 + 1, B_FORGET), jnp.float32)
    hgrn_norm_g = 1.0 + 0.05 * jax.random.normal(ks[7], (DEPTH_2, B_WIDTH), jnp.float32)
    w_o = jax.random.normal(ks[8], (DEPTH_2, D_MIX, D_MODEL), jnp.float32) * (D_MIX ** -0.5) * DEEPNORM_BETA
    ln_g = 1.0 + 0.05 * jax.random.normal(ks[9], (DEPTH_2, D_MODEL), jnp.float32)
    ln_b = 0.02 * jax.random.normal(ks[10], (DEPTH_2, D_MODEL), jnp.float32)
    return {'x': x, 'w_in': w_in, 'w_uk': w_uk, 'w_uv': w_uv, 'kv_norm_g': kv_norm_g,
            'rel_bias': rel_bias, 'lb_logits': lb_logits, 'hgrn_norm_g': hgrn_norm_g,
            'w_o': w_o, 'ln_g': ln_g, 'ln_b': ln_b}

def second_block(x, w_in, w_uk, w_uv, kv_norm_g, rel_bias, lb_logits, hgrn_norm_g, w_o, ln_g, ln_b):
    bsz, seq, _ = x.shape
    lb_all = jnp.cumsum(jax.nn.softmax(lb_logits.astype(jnp.float32), axis=0), axis=0)
    for layer in range(DEPTH_2):
        h = jnp.einsum('bsd,dc->bsc', x, w_in[layer])
        a_q, a_ckv, a_iq, a_ik, a_iw, a_gate, b_q, b_f, b_i, b_gate = jnp.split(h, SPLIT_POINTS, axis=-1)

        c = _rms_norm(a_ckv, kv_norm_g[layer])
        o_lat = _dsa_mixer(a_q.reshape(bsz, seq, A_HEADS, A_HEAD_DIM), c,
                           a_iq.reshape(bsz, seq, IDX_HEADS, IDX_DIM), a_ik, a_iw,
                           w_uk[layer], rel_bias)
        o_a = jnp.einsum('bshr,hrv->bshv', o_lat, w_uv[layer]).reshape(bsz, seq, A_WIDTH)
        o_a = o_a * jax.nn.silu(a_gate)

        o_b = _hgrn2_mixer(b_q.reshape(bsz, seq, B_HEADS, B_KEY_DIM),
                           b_f.reshape(bsz, seq, B_HEADS, B_KEY_DIM),
                           b_i.reshape(bsz, seq, B_HEADS, B_VAL_DIM), lb_all[layer])
        o_b = _rms_norm(o_b, hgrn_norm_g[layer].reshape(B_HEADS, B_VAL_DIM)).reshape(bsz, seq, B_WIDTH)
        o_b = o_b.astype(x.dtype) * jax.nn.silu(b_gate)

        y = jnp.einsum('bsc,cd->bsd', jnp.concatenate([o_a.astype(x.dtype), o_b], axis=-1), w_o[layer])
        x = _layer_norm(DEEPNORM_ALPHA * x + y, ln_g[layer], ln_b[layer])
    return x


def setup_inputs(seed=0):
    out = dict(first_inputs(seed))
    for name, value in second_inputs(seed + 1).items():
        if name != "x":
            out[name + "_2"] = value
    return out


def reference(
    x, c, positions, ada_w, ada_b, norm_g, mlp_w1, mlp_w2, gla_w_in, gla_w_a2, gla_b_a, gla_b_r,
    gla_norm_g, gla_w_o, diff_w_in, diff_lambda, diff_subln_g, diff_w_o, final_g, w_in_2,
    w_uk_2, w_uv_2, kv_norm_g_2, rel_bias_2, lb_logits_2, hgrn_norm_g_2, w_o_2, ln_g_2, ln_b_2,
):
    x = first_block(
        x, c, positions, ada_w, ada_b, norm_g, mlp_w1, mlp_w2, gla_w_in, gla_w_a2, gla_b_a,
        gla_b_r, gla_norm_g, gla_w_o, diff_w_in, diff_lambda, diff_subln_g, diff_w_o, final_g,
    )
    return second_block(
        x, w_in_2, w_uk_2, w_uv_2, kv_norm_g_2, rel_bias_2, lb_logits_2, hgrn_norm_g_2, w_o_2,
        ln_g_2, ln_b_2,
    )


_drawn_inputs = setup_inputs


def setup_inputs(seed=0):
    import zlib

    import numpy as np

    out = dict(_drawn_inputs(seed))
    spreads = {}
    factors = {'gla_b_a': 4.622,
     'gla_b_r': 8.0,
     'gla_norm_g': 5.562,
     'diff_subln_g': 5.791,
     'w_uk_2': 3.377,
     'kv_norm_g_2': 8.0,
     'rel_bias_2': 8.0,
     'lb_logits_2': 5.344,
     'hgrn_norm_g_2': 5.994,
     'ln_b_2': 2.869}
    for name, (base, spread) in spreads.items():
        noise = np.random.default_rng([zlib.crc32(name.encode()), seed]).standard_normal(out[name].shape)
        drawn = base * np.exp(spread * noise) if base else spread * noise
        out[name] = __import__('jax').numpy.asarray(drawn.astype(out[name].dtype))
    for name, factor in factors.items():
        out[name] = (out[name] * factor).astype(out[name].dtype)
    return out
```

```python
import math
from contextlib import ExitStack

import numpy as np

import concourse.bass as bass
from concourse import mybir

F = mybir.dt.float32
R = mybir.dt.float32r
B16 = mybir.dt.bfloat16
I32 = mybir.dt.int32
U32 = mybir.dt.uint32
ALU = mybir.AluOpType
ACT = mybir.ActivationFunctionType
AX = mybir.AxisListType
P = 128
T = 512
EPS = 1e-6
LN_EPS = 1e-5
LAMBDA_INIT = 0.8 - 0.6 * math.exp(-0.3)
ALPHA = 2.0 ** 0.25
NEG = -1e30
FILL = -3.0e38
TAKEN = -3.4028234663852886e38
TWO_PI = 2.0 * math.pi
C1 = 6.28125
C2 = float(np.float32(int((TWO_PI - C1) * 2 ** 22) / 2.0 ** 22))
C3 = TWO_PI - C1 - C2

VEC = {"c": (0, 8), "n00": (8, 8), "n01": (16, 8), "n10": (24, 8), "n11": (32, 8), "fin": (40, 8),
       "ada_b": (48, 96), "b_a": (144, 4), "b_r": (148, 8), "gla_g": (156, 2), "sub_g": (158, 1),
       "kv_g": (159, 1), "hg_g": (160, 4), "lb": (164, 8), "ln_g": (172, 8), "ln_b": (180, 8)}
NVEC = 188
CON = {"ident": (0, 128), "tri": (128, 128), "scan": (256, 512), "lev": (768, 7 * 128),
       "rot": (1664, 128), "adm": (1792, 128), "cau": (1920, 128), "freq": (2048, 1), "ropem": (2049, 1)}
NCON = 2050
LEVELS = (32, 16, 8, 4, 2, 1)


class Queue:

    def __init__(self, eng, sem):
        self.eng, self.sem, self.n, self.seen = eng, sem, 0, {}

    def wait(self, w):
        if w is None:
            return
        if isinstance(w, list):
            for x in w:
                self.wait(x)
            return
        s, v = w
        if v > self.seen.get(id(s), 0):
            self.eng.wait_ge(s, v)
            self.seen[id(s)] = v

    def __call__(self, fn, *waits, inc=True):
        for w in waits:
            self.wait(w)
        ins = fn(self.eng)
        if inc:
            ins.then_inc(self.sem, 1)
            self.n += 1
            return (self.sem, self.n)

    def dma(self, fn, counter, *waits):
        for w in waits:
            self.wait(w)
        counter[1] += 16
        fn(self.eng).then_inc(counter[0], 16)
        return (counter[0], counter[1])

    def now(self):
        return (self.sem, self.n)


class Slots:

    def __init__(self, bufs):
        self.bufs, self.free, self.i = bufs, [[] for _ in bufs], 0

    def take(self):
        i = self.i % len(self.bufs)
        self.i += 1
        w, self.free[i] = self.free[i], None
        assert w is not None, "taken before its release"
        return i, self.bufs[i], w

    def give(self, i, *tokens):
        self.free[i] = list(tokens)


def build(nc, D, out, debug=None):
    ctx = ExitStack()
    with ctx:
        def sb(name, shape, dt=F, c=ctx):
            return c.enter_context(nc.sbuf_tensor("sb_" + name, shape, dt))

        sem = lambda n: ctx.enter_context(nc.semaphore(n))
        SP, AC, DV, PO, PE = (Queue(e, sem(f"s_{n}")) for n, e in (
            ("sp", nc.sync), ("act", nc.scalar), ("dve", nc.vector), ("pool", nc.gpsimd), ("pe", nc.tensor)))
        counters = {}

        def cnt(name):
            if name not in counters:
                counters[name] = [sem("d_" + name), 0]
            return counters[name]

        X = sb("X", [P, 8, T])
        Hh, Hl = sb("Hh", [P, 8, T], R), sb("Hl", [P, 8, T], R)
        Oh, Ol = sb("Oh", [P, 8, T], R), sb("Ol", [P, 8, T], R)
        Wh, Wl = sb("Wh", [P, 3, 8, 128], R), sb("Wl", [P, 3, 8, 128], R)
        RAW = sb("RAW", [P, 3, 1024])
        vec = sb("vec", [P, NVEC])
        con = sb("con", [P, NCON])
        ones = sb("ones", [P, 128])
        identb = sb("identb", [P, 128], B16)
        caub = sb("caub", [P, 128], B16)
        MOD = sb("MOD", [P, 2, 48])
        SC = sb("SC", [P, 4, 8])
        cact = sb("cact", [P, 8])
        ctmp = sb("ctmp", [P, 16])
        nbr = sb("nbr", [P, 8])
        ADA = sb("ADA", [P, 2, T])
        SSQ = sb("SSQ", [P, T])
        RS = sb("RS", [P, T])
        NT = 6
        TMP = sb("TMP", [P, NT, T])
        tmp = Slots([TMP[:, i, :] for i in range(NT)])
        PS = [ctx.enter_context(nc.psum_tensor(f"PS{i}", [P, T], F)) for i in range(8)]
        pj = Slots([PS[i][:, :] for i in range(3)])
        G = [PS[3 + i][:, :] for i in range(5)]

        V = lambda n, j=0, k=1: vec[:, VEC[n][0] + j:VEC[n][0] + j + k]
        C = lambda n: con[:, CON[n][0]:CON[n][0] + CON[n][1]]
        ident = C("ident")

        t_con = SP.dma(lambda e: e.dma_start(con[:], D["con"]), cnt("con"))
        t_vec = SP.dma(lambda e: e.dma_start(vec[:], D["vec"]), cnt("vec"))
        t_x = SP.dma(lambda e: e.dma_start(X[:], D["xT"].rearrange("(c p) t -> p c t", p=P)), cnt("x"))
        t_one = DV(lambda e: e.memset(ones[:], 1.0))
        t_idb = DV(lambda e: e.tensor_copy(identb[:], ident), t_con)
        t_cau = DV(lambda e: e.tensor_copy(caub[:], C("cau")), t_con)

        raw = Slots([RAW[:, i, :] for i in range(3)])
        wsl = Slots([i for i in range(3)])

        def load(src, n=1024):
            i, buf, w = raw.take()
            t = SP.dma(lambda e: e.dma_start(buf[:, 0:n], src), cnt(f"raw{i}"), w)
            return i, buf, t

        plan, ready = [], []
        background = []

        def pump():
            if plan and len(ready) < 3:
                src, m = plan.pop(0)
                n = 8 * m
                ri, buf, t = load(src, n)
                si, _, w = wsl.take()
                view = buf[:, 0:n].rearrange("p (k m) -> p k m", k=8)
                a = AC(lambda e: e.activation(Wh[:, si, :, 0:m], view, ACT.Copy), t, w)
                b = DV(lambda e: e.tensor_tensor(Wl[:, si, :, 0:m], view, Wh[:, si, :, 0:m].bitcast(F), ALU.subtract), t, a, w)
                raw.give(ri, a, b)
                ready.append((si, m, a, b))

        def project(rhs, toks, m, *waits):
            si, bm, a, b = ready.pop(0)
            assert bm == m
            hi, lo = rhs
            bi, bank, w = pj.take()
            for k in range(8):
                for n, (ww, xx) in enumerate(((Wh, hi), (Wh, lo), (Wl, hi))):
                    last = k == 7 and n == 2
                    t = PE(lambda e, k=k, ww=ww, xx=xx, last=last, n=n: e.matmul(
                        bank[0:m, :], ww[:, si, k, 0:m], xx[:, k, :], start=(k == 0 and n == 0), stop=last),
                        *(waits if k == 0 and n == 0 else ()), w if k == 0 and n == 0 else None,
                        a if n == 0 else None, b if n == 2 else None, toks[k], inc=last)
            wsl.give(si, t)
            return bi, bank, t

        t_neg = AC(lambda e: e.activation(ctmp[:, 0:8], V("c", 0, 8), ACT.Exp, scale=-1.0), t_vec)
        t = DV(lambda e: e.tensor_scalar(ctmp[:, 8:16], ctmp[:, 0:8], 1.0, None, ALU.add), t_neg)
        t = DV(lambda e: e.reciprocal(ctmp[:, 0:8], ctmp[:, 8:16]), t)
        t_c = DV(lambda e: e.tensor_tensor(cact[:], V("c", 0, 8), ctmp[:, 0:8], ALU.mult), t)
        t_nbr = DV(lambda e: e.tensor_scalar(nbr[:], V("b_r", 0, 8), -1.0, None, ALU.mult), t_vec)
        ada_state = {"step": 0, "free": [None, None], "tok": None}
        t_mod = {}

        def ada_step():
            s = ada_state["step"]
            if s >= 96:
                return
            ada_state["step"] += 1
            layer, g, part = s // 48, s % 48 // 4, s % 4
            ri, buf, t = load(D["ada"][layer, g, part])
            acc = ADA[:, g % 2, :]
            for j in range(2):
                k = part * 2 + j
                w = buf[:, j * T:(j + 1) * T]
                if k == 0:
                    tok = DV(lambda e, w=w, k=k: e.tensor_scalar(acc, w, cact[:, k:k + 1], None, ALU.mult),
                             t, t_c, ada_state["free"][g % 2])
                else:
                    tok = DV(lambda e, w=w, k=k: e.scalar_tensor_tensor(acc, w, cact[:, k:k + 1], acc, ALU.mult, ALU.add),
                             t, ada_state["tok"])
                ada_state["tok"] = tok
            raw.give(ri, tok)
            if part == 3:
                bi, bank, w = pj.take()
                for c in range(4):
                    tp = PE(lambda e, c=c: e.matmul(bank[:, c:c + 1], acc[:, c * 128:(c + 1) * 128], ones[:, 0:1],
                                                    start=True, stop=True), tok, w, t_one, inc=c == 3)
                ada_state["free"][g % 2] = tp
                tm = DV(lambda e: e.tensor_tensor(MOD[:, layer, g * 4:g * 4 + 4], bank[:, 0:4],
                                                  V("ada_b", layer * 48 + g * 4, 4), ALU.add), tp, t_vec)
                pj.give(bi, tm)
                t_mod[layer, g] = tm
                if g in (3, 9):
                    which = 0 if g == 3 else 1
                    sl = SC[:, layer * 2 + which, :]
                    t_mod[layer, "A", which] = DV(lambda e: e.scalar_tensor_tensor(
                        sl, MOD[:, layer, g * 4 - 4:g * 4 + 4], 1.0, V(f"n{layer}{which}", 0, 8), ALU.add, ALU.mult),
                        tm, t_mod[layer, g - 1])

        ssq_free = [None]

        def ssq_add(j, xtok):
            if j == 0:
                t = AC(lambda e: e.activation(SSQ[:], X[:, 0, :], ACT.Square), xtok, ssq_free[0])
            else:
                i, buf, w = tmp.take()
                a = AC(lambda e: e.activation(buf, X[:, j, :], ACT.Square), xtok, w)
                t = PO(lambda e: e.tensor_tensor(SSQ[:], SSQ[:], buf, ALU.add), a, ssq_free[1])
                tmp.give(i, t)
            ssq_free[1:] = [t]
            return t

        def rstd_of(bank, tok, dst, n, eps, *waits):
            a = AC(lambda e: e.activation(dst, bank, ACT.Ln, scale=1.0 / n, bias=epsb[:, 0:1]), tok, *waits)
            return AC(lambda e: e.activation(dst, dst, ACT.Exp, scale=-0.5), a)

        epsb = sb("epsb", [P, 2])
        t_eps = DV(lambda e: e.memset(epsb[:, 0:1], EPS))
        t_eps2 = DV(lambda e: e.memset(epsb[:, 1:2], LN_EPS))

        def norm(toks, h_free, A=None, Bc=None, ab=(), g=None):
            bi, bank, w = pj.take()
            tp = PE(lambda e: e.matmul(bank, ones[:], SSQ[:], start=True, stop=True), toks, w, t_one)
            ssq_free[0] = tp
            tr = rstd_of(bank, tp, RS[:], 1024, EPS, t_eps)
            pj.give(bi, tr)
            res = []
            for j in range(8):
                if g is None:
                    i, buf, w = tmp.take()
                    x1 = DV(lambda e, j=j, buf=buf: e.tensor_tensor(buf, X[:, j, :], RS[:], ALU.mult), tr, w, t_x)
                    a = AC(lambda e, j=j, buf=buf: e.activation(Hh[:, j, :], buf, ACT.Identity, scale=A[:, j:j + 1],
                                                                bias=Bc[:, j:j + 1]), x1, h_free, *ab)
                    i2, buf2, w2 = tmp.take()
                    x2 = DV(lambda e, j=j, buf=buf, buf2=buf2: e.tensor_scalar(buf2, buf, A[:, j:j + 1], Bc[:, j:j + 1],
                                                                              ALU.mult, ALU.add), x1, w2, *ab)
                    b = DV(lambda e, j=j, buf2=buf2: e.tensor_tensor(Hl[:, j, :], buf2, Hh[:, j, :].bitcast(F),
                                                                     ALU.subtract), x2, a, h_free)
                    tmp.give(i, a, x2)
                    tmp.give(i2, b)
                else:
                    x1 = DV(lambda e, j=j: e.scalar_tensor_tensor(X[:, j, :], X[:, j, :], V(g, j), RS[:], ALU.mult,
                                                                  ALU.mult), tr, t_vec)
                    a = AC(lambda e, j=j: e.activation(Hh[:, j, :], X[:, j, :], ACT.Copy), x1, h_free)
                    b = DV(lambda e, j=j: e.tensor_tensor(Hl[:, j, :], X[:, j, :], Hh[:, j, :].bitcast(F),
                                                          ALU.subtract), x1, a, h_free)
                res.append([a, b])
            return res

        def residual(gate, j, bi, bank, tp, g_tok, last):
            t = DV(lambda e: e.scalar_tensor_tensor(X[:, j, :], bank, gate[:, j:j + 1], X[:, j, :], ALU.mult, ALU.add),
                   tp, g_tok, t_x)
            pj.give(bi, t)
            return ssq_add(j, t) if last else t

        def split_out(src, hi, lo, src_tok, *waits):
            a = AC(lambda e: e.activation(hi, src, ACT.Copy), src_tok, *waits)
            b = DV(lambda e: e.tensor_tensor(lo, src, hi.bitcast(F), ALU.subtract), src_tok, a, *waits)
            return [a, b]

        def transposes(src, tok, *waits):
            bi, bank, w = pj.take()
            for i in range(4):
                tp = PE(lambda e, i=i: e.transpose(bank[:, i * 128:(i + 1) * 128], src[:, i * 128:(i + 1) * 128], ident),
                        tok, w, t_con, *waits, inc=i == 3)
            return bi, bank, tp

        def mlp(layer, h_toks):
            gate = MOD[:, layer, 40:48]
            o_free = None
            for g in range(4):
                o_toks = []
                for c in range(8):
                    bi, bank, tp = project((Hh, Hl), h_toks, 128)
                    i, r, w = tmp.take()
                    a = AC(lambda e, r=r, bank=bank: e.activation(r, bank, ACT.Relu), tp, w)
                    pj.give(bi, a)
                    hi = AC(lambda e, r=r, c=c: e.activation(Oh[:, c, :], r, ACT.Square), a, o_free)
                    i2, q, w2 = tmp.take()
                    s = DV(lambda e, r=r, q=q: e.tensor_tensor(q, r, r, ALU.mult), a, w2)
                    lo = DV(lambda e, q=q, c=c: e.tensor_tensor(Ol[:, c, :], q, Oh[:, c, :].bitcast(F), ALU.subtract),
                            s, hi, o_free)
                    tmp.give(i, hi, s)
                    tmp.give(i2, lo)
                    o_toks.append([hi, lo])
                    h_last = tp
                    pump()
                    ada_step()
                for d in range(8):
                    bi, bank, tp = project((Oh, Ol), o_toks, 128)
                    o_free = tp
                    t = residual(gate, d, bi, bank, tp, [t_mod[layer, 10], t_mod[layer, 11]], g == 3)
                    pump()
                    ada_step()
            return t, h_last, o_free

        def linear_attention(S, s_free, nh, nv, qd, q_tok, scores, ksT, ks_tok, vT, v_tok, dec, dec_tok, finish):
            W = nv * 128
            per = T // W
            ub = [G[0], G[1]]
            ob = [G[2], G[3]]
            u_free = [None, None]
            o_free = None
            s_free = [s_free] * 3
            st = [None] * 9
            for t in range(4):
                sc, sc_tok = scores(t)
                for n in (2 * t, 2 * t + 1):
                    if n == 7:
                        continue
                    lo = 64 * (n % 2)
                    tp = []
                    for h in range(nh):
                        b, o = h // per, (h % per) * W
                        tp.append(PE(lambda e, h=h, b=b, o=o, lo=lo, t=t: e.matmul(
                            ub[b][:, o:o + W], ksT[lo:lo + 64, t, h, :], vT[lo:lo + 64, t, h * W:(h + 1) * W],
                            start=True, stop=True), u_free[b], ks_tok, v_tok, inc=h % per == per - 1 or h == nh - 1))
                    new, old = S[:, (n + 1) % 3], S[:, n % 3]
                    tp = [[x for x in tp[h // per * per:h // per * per + per] if x] for h in range(nh)]
                    for h in range(nh):
                        b, o = h // per, (h % per) * W
                        if n == 0:
                            x = DV(lambda e, h=h, b=b, o=o, new=new: e.tensor_copy(new[:, h, :], ub[b][:, o:o + W]),
                                   tp[h], s_free[(n + 1) % 3])
                        else:
                            x = DV(lambda e, h=h, b=b, o=o, new=new, old=old, n=n: e.scalar_tensor_tensor(
                                new[:, h, :], old[:, h, :], dec[:, h, n:n + 1], ub[b][:, o:o + W], ALU.mult, ALU.add),
                                tp[h], st[n], dec_tok, s_free[(n + 1) % 3])
                        u_free[b] = x
                    st[n + 1] = x
                for v in range(nv):
                    for h in range(nh):
                        dst = ob[v][:, h * 128:(h + 1) * 128]
                        c0 = h * W + v * 128
                        jobs = [(dst, vT[:, t, c0:c0 + 128], sc[:, h, :], [sc_tok, v_tok, o_free])]
                        for n in (2 * t, 2 * t + 1):
                            if n > 0:
                                u = 64 * (n % 2)
                                jobs.append((dst[:, u:u + 64], S[:, n % 3, h, v * 128:(v + 1) * 128],
                                             qd[:, h, n * 64:(n + 1) * 64], [st[n], q_tok]))
                        for m, (o, l, r, w) in enumerate(jobs):
                            tp = PE(lambda e, o=o, l=l, r=r, m=m, k=len(jobs): e.matmul(o, l, r, start=m == 0, stop=m == k - 1),
                                    w, inc=m == len(jobs) - 1)
                s_free = [tp] * 3
                o_free = finish(t, ob, tp)

        wt = lambda name, *ix: D[name][ix] if ix else D[name]
        plan.append((D["w_a"], 16))
        for h in range(4):
            plan += [(D["gla_in"][4 + h], 128), (D["gla_in"][h], 128)]
        plan += [(D["gla_in"][8 + j], 128) for j in range(16)]
        plan += [(D["gla_wo"][j], 128) for j in range(8)]
        for g in range(4):
            plan += [(D["w1_0"][g * 8 + c], 128) for c in range(8)]
            plan += [(D["w2_0"][g * 8 + c], 128) for c in range(8)]
        plan += [(D["diff_in"][16 + j], 128) for j in range(8)]
        for h in range(8):
            plan += [(D["diff_in"][h], 128), (D["diff_in"][8 + h], 128)]
        plan += [(D["diff_wo"][j], 128) for j in range(8)]
        for g in range(4):
            plan += [(D["w1_1"][g * 8 + c], 128) for c in range(8)]
            plan += [(D["w2_1"][g * 8 + c], 128) for c in range(8)]

        plan += [(D["in_iq"][j], 128) for j in range(4)] + [(D["in_ik"], 72), (D["in_c"][0], 128)]
        plan += [(D["in_b"][4 + j], 128) for j in range(4)] + [(D["in_b"][j], 128) for j in range(4)]
        plan += [(D["in_b"][8 + j], 128) for j in range(4)]
        for h in range(4):
            plan += [(D["in_q"][h], 128), (D["in_ag"][h], 128), (D["in_b"][12 + h], 128)]
        plan += [(D["wo_2"][j], 128) for j in range(8)]

        for j in range(8):
            t_ss = ssq_add(j, t_x)
        for _ in range(16):
            ada_step()
        for _ in range(3):
            pump()
        h_toks = norm(t_ss, None, SC[:, 0, :], MOD[:, 0, 0:8], (t_mod[0, "A", 0], t_mod[0, 0], t_mod[0, 1]))

        with ExitStack() as ph:
            qd = sb("qd", [P, 4, T], c=ph)
            ki = sb("ki", [P, 4, T], c=ph)
            ksT = sb("ksT", [P, 4, 4, 128], c=ph)
            vT = sb("vT", [P, 4, 1024], c=ph)
            rg = sb("rg", [P, 8, T], c=ph)
            EX = sb("EX", [P, 2, 3, T], c=ph)
            dec = sb("dec", [P, 4, 8], c=ph)
            al = sb("al", [16, T], c=ph)
            wa2 = sb("wa2", [16, T], c=ph)
            t_wa2 = SP.dma(lambda e: e.dma_start(wa2[:], D["w_a2"]), cnt("wa2"))
            bi, bank, tp = project((Hh, Hl), h_toks, 16)
            t_al = AC(lambda e: e.activation(al[:], bank[0:16, :], ACT.Copy), tp)
            pj.give(bi, t_al)
            pump()
            ada_step()
            ex_free = [[None], [None]]
            ki_tok, q_tok, ks_tok, d_tok = [], [], [], []
            for h in range(4):
                zi, z, w = pj.take()
                tz = PE(lambda e: e.matmul(z, wa2[:, h * 128:(h + 1) * 128], al[:], start=True, stop=True), t_wa2, t_al, w)
                EB, EN, EK = (EX[:, h % 2, i, :] for i in range(3))
                i1, a1, w1 = tmp.take()
                i2, a2, w2 = tmp.take()
                ta = AC(lambda e: e.activation(a1, z, ACT.Abs, bias=V("b_a", h)), tz, w1, t_vec)
                tm = DV(lambda e: e.tensor_scalar(a2, z, V("b_a", h), 0.0, ALU.add, ALU.min), tz, ta, w2, t_vec)
                pj.give(zi, ta, tm)
                ta = AC(lambda e: e.activation(a1, a1, ACT.Exp, scale=-1.0), ta)
                ta = AC(lambda e: e.activation(a1, a1, ACT.Ln, bias=1.0), ta)
                tm = DV(lambda e: e.tensor_tensor(a2, a2, a1, ALU.subtract), tm, ta)
                tb = DV(lambda e: e.tensor_tensor_scan(a1, C("scan"), a2, 0.0, ALU.mult, ALU.add), tm, t_con)
                tB = AC(lambda e: e.activation(EB, a1, ACT.Exp, scale=1.0 / 16), tb, ex_free[h % 2])
                tN = AC(lambda e: e.activation(EN, a1, ACT.Exp, scale=-1.0 / 16), tb)
                a13 = a1.rearrange("p (n c) -> p n c", c=64)
                a23 = a2.rearrange("p (n c) -> p n c", c=64)
                td = DV(lambda e: e.tensor_tensor(a23, a13, a13[:, :, 63:64].to_broadcast([P, 8, 64]), ALU.subtract), tb)
                tK = AC(lambda e: e.activation(EK, a2, ACT.Exp, scale=-1.0 / 16), td)
                dtok = DV(lambda e: e.tensor_copy(dec[:, h, :], EB.rearrange("p (n c) -> p n c", c=64)[:, :, 63]), tB)
                d_tok.append(dtok)
                tmp.give(i1, tB, tN, td)
                tmp.give(i2, tK)
                bi, bank, tp = project((Hh, Hl), h_toks, 128)
                i3, kst, w3 = tmp.take()
                x1 = DV(lambda e: e.tensor_tensor(kst, bank, EK, ALU.mult), tp, tK, w3)
                x2 = DV(lambda e: e.tensor_tensor(ki[:, h, :], bank, EN, ALU.mult), tN)
                pj.give(bi, x2)
                ki_tok.append(x2)
                pump()
                ada_step()
                bi, bank, tp = project((Hh, Hl), h_toks, 128)
                x3 = DV(lambda e: e.scalar_tensor_tensor(qd[:, h, :], bank, 128.0 ** -0.5, EB, ALU.mult, ALU.mult), tp, tB)
                pj.give(bi, x3)
                q_tok.append(x3)
                ex_free[h % 2] = [x1, x2, x3, dtok]
                bi, bank, tp = transposes(kst, x1)
                tmp.give(i3, tp)
                a = AC(lambda e: e.activation(ksT[:, :, h, :], bank.rearrange("p (a b) -> p a b", a=4), ACT.Copy), tp)
                pj.give(bi, a)
                ks_tok.append(a)
                pump()
                ada_step()
            v_tok = []
            for j in range(8):
                bi, bank, tp = project((Hh, Hl), h_toks, 128)
                i1, a1, w1 = tmp.take()
                a = AC(lambda e, a1=a1, bank=bank: e.activation(a1, bank, ACT.Copy), tp, w1)
                pj.give(bi, a)
                bi, bank, tp = transposes(a1, a)
                tmp.give(i1, tp)
                a = AC(lambda e, bank=bank, j=j: e.activation(vT[:, :, j * 128:(j + 1) * 128],
                                                              bank.rearrange("p (a b) -> p a b", a=4), ACT.Copy), tp)
                pj.give(bi, a)
                v_tok.append(a)
                pump()
                ada_step()
            r_tok = []
            for j in range(8):
                bi, bank, tp = project((Hh, Hl), h_toks, 128)
                i1, a1, w1 = tmp.take()
                a = AC(lambda e, a1=a1, bank=bank, j=j: e.activation(a1, bank, ACT.Exp, scale=-1.0, bias=nbr[:, j:j + 1]),
                       tp, w1, t_nbr)
                x = DV(lambda e, a1=a1: e.tensor_scalar(a1, a1, 1.0, None, ALU.add), a)
                x = DV(lambda e, a1=a1: e.reciprocal(a1, a1), x)
                x = DV(lambda e, a1=a1, bank=bank, j=j: e.scalar_tensor_tensor(rg[:, j, :], bank, V("b_r", j), a1,
                                                                               ALU.add, ALU.mult), x, tp)
                pj.give(bi, x, a)
                tmp.give(i1, x)
                r_tok.append(x)
                h_last = tp
                pump()
                ada_step()
            S = EX[:, :, :, :].rearrange("p a b t -> p (a b t)").rearrange("p (s h v) -> p s h v", s=3, h=4)
            tri = C("tri").unsqueeze(1).to_broadcast([P, 4, 128])

            def scores(t):
                bi, bank, w = pj.take()
                for h in range(4):
                    tp = PE(lambda e, h=h: e.matmul(bank[:, h * 128:(h + 1) * 128], ki[:, h, t * 128:(t + 1) * 128],
                                                    qd[:, h, t * 128:(t + 1) * 128], start=True, stop=True),
                            w, ki_tok, q_tok, inc=h == 3)
                sc = ki[:, :, t * 128:(t + 1) * 128]
                x = DV(lambda e: e.tensor_tensor(sc, bank.rearrange("p (h s) -> p h s", h=4), tri, ALU.mult), tp)
                pj.give(bi, x)
                return sc, x

            o_toks = []

            def finish(t, ob, tp):
                bufs = [tmp.take() for _ in range(2)]
                sq = [AC(lambda e, v=v: e.activation(bufs[v][1], ob[v], ACT.Square), tp, bufs[v][2]) for v in range(2)]
                s = PO(lambda e: e.tensor_tensor(bufs[0][1], bufs[0][1], bufs[1][1], ALU.add), sq[0], sq[1])
                bi, bank, w = pj.take()
                m = PE(lambda e: e.matmul(bank, ones[:], bufs[0][1], start=True, stop=True), s, w)
                tmp.give(bufs[0][0], m)
                i3, rs, w3 = tmp.take()
                tr = rstd_of(bank, m, rs, 256, EPS, w3)
                pj.give(bi, tr)
                xs = []
                for v in range(2):
                    i4, on, w4 = (bufs[1][0], bufs[1][1], s) if v == 0 else tmp.take()
                    x = DV(lambda e, v=v, on=on: e.scalar_tensor_tensor(on, ob[v], V("gla_g", v), rs, ALU.mult, ALU.mult),
                           tr, w4, t_vec, tp, sq[v])
                    free = x
                    rv = rg[:, :, t * 128:(t + 1) * 128].rearrange("p (h v) s -> p v h s", v=2)[:, v]
                    o3 = on.rearrange("p (h s) -> p h s", h=4)
                    x = DV(lambda e, rv=rv, o3=o3: e.tensor_tensor(o3, o3, rv, ALU.mult), x, r_tok)
                    hv = Oh[:, :, t * 128:(t + 1) * 128].rearrange("p (h v) s -> p v h s", v=2)[:, v]
                    lv = Ol[:, :, t * 128:(t + 1) * 128].rearrange("p (h v) s -> p v h s", v=2)[:, v]
                    both = split_out(o3, hv, lv, x)
                    tmp.give(i4, *both)
                    xs += both
                    free2 = free
                tmp.give(i3, free2)
                o_toks.extend(xs)
                return [free2, sq]

            linear_attention(S, ex_free[0] + ex_free[1], 4, 2, qd, q_tok, scores, ksT, ks_tok, vT, v_tok, dec, d_tok, finish)
            mix_done = [PE.now(), AC.now(), DV.now(), PO.now()]

        def wo(rhs_toks, gate, g_tok):
            for j in range(8):
                bi, bank, tp = project((Oh, Ol), [rhs_toks] * 8, 128)
                t = residual(gate, j, bi, bank, tp, g_tok, True)
                pump()
                ada_step()
            return t, tp

        t_ss, o_last = wo(o_toks, MOD[:, 0, 16:24], [t_mod[0, 4], t_mod[0, 5]])
        h_toks = norm(t_ss, h_last, SC[:, 1, :], MOD[:, 0, 24:32], (t_mod[0, "A", 1], t_mod[0, 6], t_mod[0, 7]))
        t_ss, h_last, o_last = mlp(0, h_toks)
        h_toks = norm(t_ss, h_last, SC[:, 2, :], MOD[:, 1, 0:8], (t_mod[1, "A", 0], t_mod[1, 0], t_mod[1, 1]))

        if debug == 1:
            SP.dma(lambda e: e.dma_start(out, X[:]), cnt("out"), t_ss)
            SP.wait((counters["out"][0], counters["out"][1]))
            return

        with ExitStack() as ph:
            vT = sb("dvT", [P, 4, 1024], c=ph)
            RC, RSn = sb("ropec", [P, T], c=ph), sb("ropes", [P, T], c=ph)
            QK = sb("QK", [P, 2, 2, T], c=ph)
            WK = sb("WK", [P, 12, T], c=ph)
            wk = Slots([WK[:, i, :] for i in range(12)])
            st = sb("st", [P, 8, 8], c=ph)
            lamb = sb("lamb", [P, 256], c=ph)
            lam2 = sb("lam2", [P, 8], c=ph)
            posi = sb("posi", [P, T], I32, c=ph)
            t_pos = SP.dma(lambda e: e.dma_start(posi[:], D["pos"].to_broadcast([P, T])), cnt("pos"), mix_done)
            t_lam = SP.dma(lambda e: e.dma_start(lamb[:], D["lam"].to_broadcast([P, 256])), cnt("lam"), mix_done)
            for q in (AC, DV, PO, PE):
                q.wait(mix_done)

            l4 = lamb[:].rearrange("p (a b d) -> p a b d", a=2, b=2)
            t = DV(lambda e: e.tensor_tensor(l4[:, :, 0, :], l4[:, :, 0, :], l4[:, :, 1, :], ALU.mult), t_lam)
            t = DV(lambda e: e.reduce_sum(lam2[:, 0:2], l4[:, :, 0, :], axis=AX.X), t)
            t = AC(lambda e: e.activation(lam2[:, 2:4], lam2[:, 0:2], ACT.Exp), t)
            t = DV(lambda e: e.tensor_tensor(lam2[:, 4:5], lam2[:, 3:4], lam2[:, 2:3], ALU.subtract), t)
            t_nl = DV(lambda e: e.tensor_scalar(lam2[:, 5:6], lam2[:, 4:5], -LAMBDA_INIT, None, ALU.add), t)
            nlam = lam2[:, 5:6]
            t_sg = DV(lambda e: e.tensor_scalar(lam2[:, 6:7], V("sub_g"), 1.0 - LAMBDA_INIT, None, ALU.mult))
            subg = lam2[:, 6:7]

            (i1, ang, w1), (i2, nn, w2) = wk.take(), wk.take()
            t = DV(lambda e: e.tensor_copy(ang, posi[:]), t_pos)
            t = DV(lambda e: e.tensor_scalar(ang, ang, C("freq"), None, ALU.mult), t)
            t = DV(lambda e: e.tensor_scalar(nn, ang, 1.0 / TWO_PI, 12582912.0, ALU.mult, ALU.add), t)
            t = DV(lambda e: e.tensor_scalar(nn, nn, -12582912.0, None, ALU.add), t)
            for c in (C1, C2, C3):
                t = DV(lambda e, c=c: e.scalar_tensor_tensor(ang, nn, -c, ang, ALU.mult, ALU.add), t)
            t = DV(lambda e: e.tensor_scalar(ang, ang, 3.1415925, -3.1415925, ALU.min, ALU.max), t)
            ts = AC(lambda e: e.activation(RSn[:], ang, ACT.Sin), t)
            t = DV(lambda e: e.scalar_tensor_tensor(nn, ang, -1.0, ang, ALU.mult, ALU.max), t)
            t = DV(lambda e: e.tensor_scalar(nn, nn, -1.0, math.pi / 2, ALU.mult, ALU.add), t)
            tc = AC(lambda e: e.activation(RC[:], nn, ACT.Sin), t)
            t_rope = [ts, tc]
            wk.give(i1, ts, t)
            wk.give(i2, tc)

            v_tok = []
            for j in range(8):
                bi, bank, tp = project((Hh, Hl), h_toks, 128)
                i1, a1, w1 = tmp.take()
                a = AC(lambda e: e.activation(a1, bank, ACT.Copy), tp, w1)
                pj.give(bi, a)
                bi, bank, tp = transposes(a1, a)
                tmp.give(i1, tp)
                a = AC(lambda e: e.activation(vT[:, :, j * 128:(j + 1) * 128],
                                              bank.rearrange("p (a b) -> p a b", a=4), ACT.Copy), tp)
                pj.give(bi, a)
                v_tok.append(a)
                pump()

            qk_free = [None, None]

            def rope(dst, bi, bank, tp, scale, free):
                i1, q, w1 = wk.take()
                a = AC(lambda e: e.activation(q, bank, ACT.Copy, scale=scale), tp, w1)
                pj.give(bi, a)
                bi, bank, w = pj.take()
                tr = PE(lambda e: e.matmul(bank, C("rot"), q, start=True, stop=True), a, w, t_con)
                i2, q2, w2 = wk.take()
                x1 = PO(lambda e: e.tensor_tensor(q2, q, RC[:], ALU.mult), a, t_rope, w2)
                wk.give(i1, tr, x1)
                i3, q3, w3 = wk.take()
                x2 = DV(lambda e: e.tensor_tensor(q3, bank, RSn[:], ALU.mult), tr, t_rope, w3)
                pj.give(bi, x2)
                x3 = DV(lambda e: e.tensor_tensor(dst, q2, q3, ALU.add), x1, x2, free)
                wk.give(i2, x3)
                wk.give(i3, x3)
                return x3

            g_free = [None, None]
            o_free = [None]
            blk = {}

            def att_scores(h, i, qk_tok):
                L = 128 * (i + 1)
                sl = st[:, (h * 4 + i) % 8, :]
                pair = i % 2
                ps, ex = [], []
                for m in range(2):
                    g = G[2 * pair + m]
                    r = slice(64 * m, 64 * m + 64)
                    PE(lambda e: e.matmul(g[:, 0:L], QK[r, h % 2, 0, i * 128:(i + 1) * 128], QK[r, h % 2, 1, 0:L],
                                          start=True, stop=False), qk_tok, g_free[pair], inc=False)
                    tp = PE(lambda e: e.matmul(g[:, L - 128:L], identb[:], caub[:], start=False, stop=True), t_idb, t_cau)
                    tm = DV(lambda e: e.reduce_max(sl[:, m:m + 1], g[:, 0:L], axis=AX.X, negate=True), tp)
                    pi, p, w = wk.take()
                    te = AC(lambda e: e.activation(p[:, 0:L], g[:, 0:L], ACT.Exp, bias=sl[:, m:m + 1],
                                                   accum_out=sl[:, 2 + m:3 + m]), tm, w)
                    ps.append((pi, p))
                    ex.append(te)
                g_free[pair] = ex[1]
                qk_free[h % 2] = tp
                t = DV(lambda e: e.reciprocal(sl[:, 4:6], sl[:, 2:4]), ex[0], ex[1])
                t2 = DV(lambda e: e.tensor_tensor(sl[:, 6:7], sl[:, 5:6], nlam, ALU.mult), t, t_nl)
                p0, p1 = ps[0][1], ps[1][1]
                t = DV(lambda e: e.tensor_scalar(p0[:, 0:L], p0[:, 0:L], sl[:, 4:5], None, ALU.mult), t)
                t = DV(lambda e: e.scalar_tensor_tensor(p1[:, 0:L], p1[:, 0:L], sl[:, 6:7], p0[:, 0:L], ALU.mult, ALU.add),
                       t, t2)
                wk.give(ps[0][0], t)
                blk[h, i] = (ps[1][0], p1, t)

            def att_turn(h, i):
                pi, p, t = blk.pop((h, i))
                bi, bank, w = pj.take()
                for s in range(i + 1):
                    tp = PE(lambda e: e.transpose(bank[:, s * 128:(s + 1) * 128], p[:, s * 128:(s + 1) * 128], ident),
                            t, w, inc=s == i)
                wk.give(pi, tp)
                ai, aT, w = wk.take()
                a = AC(lambda e: e.activation(aT[:, 0:128 * (i + 1)], bank[:, 0:128 * (i + 1)], ACT.Copy), tp, w)
                pj.give(bi, a)
                blk[h, i, "T"] = (ai, aT, a)

            def att_values(h, i):
                ai, aT, a = blk.pop((h, i, "T"))
                for s in range(i + 1):
                    tp = PE(lambda e: e.matmul(G[4][:, i * 128:(i + 1) * 128], vT[:, s, h * 128:(h + 1) * 128],
                                               aT[:, s * 128:(s + 1) * 128], start=s == 0, stop=s == i),
                            a, v_tok, o_free[0], inc=s == i)
                wk.give(ai, tp)
                return tp

            o_toks = []

            def att_out(h, tp):
                i1, sq, w1 = wk.take()
                a = AC(lambda e: e.activation(sq, G[4], ACT.Square), tp, w1)
                bi, bank, w = pj.take()
                m = PE(lambda e: e.matmul(bank, ones[:], sq, start=True, stop=True), a, w)
                tr = rstd_of(bank, m, sq, 128, EPS)
                pj.give(bi, tr)
                i2, on, w2 = wk.take()
                x = DV(lambda e: e.scalar_tensor_tensor(on, G[4], subg, sq, ALU.mult, ALU.mult), tr, w2, t_sg)
                o_free[0] = x
                wk.give(i1, x)
                both = split_out(on, Oh[:, h, :], Ol[:, h, :], x, o_last)
                wk.give(i2, *both)
                o_toks.append(both)

            for h in range(9):
                if h > 0:
                    att_scores(h - 1, 3, qk_tok)
                    att_scores(h - 1, 2, qk_tok)
                if h < 8:
                    bi, bank, tp = project((Hh, Hl), h_toks, 128)
                    xq = rope(QK[:, h % 2, 0, :], bi, bank, tp, 0.125, qk_free[h % 2])
                    pump()
                if h > 0:
                    att_turn(h - 1, 3)
                    att_turn(h - 1, 2)
                    att_scores(h - 1, 1, qk_tok)
                    att_scores(h - 1, 0, qk_tok)
                if h < 8:
                    bi, bank, tp = project((Hh, Hl), h_toks, 128)
                    h_last = tp
                    xk = rope(QK[:, h % 2, 1, :], bi, bank, tp, 1.0, qk_free[h % 2])
                    pump()
                if h > 0:
                    att_values(h - 1, 3)
                    att_values(h - 1, 2)
                    att_turn(h - 1, 1)
                    att_turn(h - 1, 0)
                    att_values(h - 1, 1)
                    att_out(h - 1, att_values(h - 1, 0))
                qk_tok = [xq, xk]
            mix_done = [PE.now(), AC.now(), DV.now(), PO.now()]

        flat = [t for both in o_toks for t in both]
        t_ss, o_last = wo(flat, MOD[:, 1, 16:24], [t_mod[1, 4], t_mod[1, 5]])
        if debug == 2:
            SP.dma(lambda e: e.dma_start(out, X[:]), cnt("out"), t_ss)
            SP.wait((counters["out"][0], counters["out"][1]))
            return
        h_toks = norm(t_ss, h_last, SC[:, 3, :], MOD[:, 1, 24:32], (t_mod[1, "A", 1], t_mod[1, 6], t_mod[1, 7]))
        t_ss, h_last, o_last = mlp(1, h_toks)
        if debug == 3:
            SP.dma(lambda e: e.dma_start(out, X[:]), cnt("out"), t_ss)
            SP.wait((counters["out"][0], counters["out"][1]))
            return
        h_toks = norm(t_ss, h_last, g="fin")

        with ExitStack() as ph:
            SEL = sb("SEL", [P, 1152], c=ph)
            MKP = sb("MK", [P, 1280], c=ph)
            MK = [MKP[:, 64 * i * (i + 1):64 * (i + 1) * (i + 2)] for i in range(4)]
            cT, ctok = sb("cT", [P, T], c=ph), sb("ctok", [P, 4, 128], c=ph)
            K, Q, Bc, FB, SH, ksT, vT = (sb(n, [P, 4, T], c=ph) for n in ("K2", "Q2", "B2", "FB", "SH", "ksT2", "vT2"))
            iwt, m8 = sb("iwt", [P, 4, 8], c=ph), sb("m8", [P, 3, 8], c=ph)
            dec = sb("dec2", [P, 4, 8], c=ph)
            lb2 = sb("lb2", [P, 6, 4], c=ph)
            st = sb("st2", [P, 4, 4], c=ph)
            wuk, wuv = sb("wuk", [P, 4, 128], c=ph), sb("wuv", [P, 4, 128], c=ph)
            relb = sb("relb", [32, 4], c=ph)
            scr = nc.dram_tensor("scr", (4, 128, 640), F, kind="Internal").ap()
            for q in (SP, AC, DV, PO, PE):
                q.wait(mix_done)
            SL = {1: (0, 256), 2: (256, 384), 3: (640, 512)}
            sel = {i: SEL[:, o:o + n] for i, (o, n) in SL.items()}
            t_uk = SP.dma(lambda e: e.dma_start(wuk[:], D["w_uk"].rearrange("p (h r) -> p h r", h=4)), cnt("wuk"))
            t_uv = SP.dma(lambda e: e.dma_start(wuv[:], D["w_uv"].rearrange("p (h r) -> p h r", h=4)), cnt("wuv"))
            t_rel = SP.dma(lambda e: e.dma_start(relb[:], D["rel"]), cnt("rel"))
            ada = ADA[:].rearrange("p a t -> p (a t)")
            hot = ada[0:32, 0:640]
            t_hot = SP.dma(lambda e: e.dma_start(hot, D["hot"]), cnt("hot"), mix_done)

            rb = SH[0:32, 0, :].rearrange("p (h m) -> p h m", h=4)
            t_rb = DV(lambda e: e.tensor_copy(rb, relb[:].unsqueeze(2).to_broadcast([32, 4, 128])), t_rel)
            t_scr = []
            for h in range(4):
                for o, n in ((0, 512), (512, 128)):
                    bi, bank, w = pj.take()
                    tp = PE(lambda e: e.matmul(bank[:, 0:n], rb[:, h, :], hot[:, o:o + n], start=True, stop=True),
                            t_rb, t_hot, w)
                    i1, a1, w1 = tmp.take()
                    a = AC(lambda e: e.activation(a1[:, 0:n], bank[:, 0:n], ACT.Copy), tp, w1)
                    pj.give(bi, a)
                    t = SP.dma(lambda e: e.dma_start(scr[h][:, o:o + n], a1[:, 0:n]), cnt(f"scr{h}{o}"), a)
                    tmp.give(i1, t)
                    t_scr.append(t)

            l0, l1 = V("lb", 0, 4), V("lb", 4, 4)
            t = DV(lambda e: e.tensor_tensor(lb2[:, 0, :], l0, l1, ALU.max))
            ta = DV(lambda e: e.tensor_tensor(lb2[:, 1, :], l0, lb2[:, 0, :], ALU.subtract), t)
            tb = DV(lambda e: e.tensor_tensor(lb2[:, 2, :], l1, lb2[:, 0, :], ALU.subtract), t)
            t = AC(lambda e: e.activation(lb2[:, 1:3, :], lb2[:, 1:3, :], ACT.Exp), ta, tb)
            t = DV(lambda e: e.tensor_tensor(lb2[:, 3, :], lb2[:, 1, :], lb2[:, 2, :], ALU.add), t)
            t = DV(lambda e: e.reciprocal(lb2[:, 3, :], lb2[:, 3, :]), t)
            t = DV(lambda e: e.tensor_tensor(lb2[:, 4, :], lb2[:, 1, :], lb2[:, 3, :], ALU.mult), t)
            t_lb = DV(lambda e: e.tensor_scalar(lb2[:, 5, :], lb2[:, 4, :], -1.0, 1.0, ALU.mult, ALU.add), t)
            lb, oml = lb2[:, 4, :], lb2[:, 5, :]

            iq_tok = []
            for j in range(4):
                bi, bank, tp = project((Hh, Hl), h_toks, 128)
                a = AC(lambda e: e.activation(Q[:, j, :], bank, ACT.Copy), tp)
                pj.give(bi, a)
                iq_tok.append(a)
                pump()
            ik = FB[:, 0, :]
            bi, bank, tp = project((Hh, Hl), h_toks, 72)
            a1 = AC(lambda e: e.activation(ik[0:64, :], bank[0:64, :], ACT.Copy), tp)
            a2 = AC(lambda e: e.activation(FB[64:72, 1, :], bank[64:72, :], ACT.Copy), tp)
            pj.give(bi, a2)
            pump()
            t_ik = SP.dma(lambda e: e.dma_start(ik[64:128, :], ik[0:64, :]), cnt("ik"), a1)
            bi, bank, w = pj.take()
            for i in range(4):
                tp = PE(lambda e: e.transpose(bank[:, i * 8:(i + 1) * 8], FB[64:72, 1, i * 128:(i + 1) * 128],
                                              ident[64:72, 64:72]), a2, w, inc=i == 3)
            t_iw = DV(lambda e: e.tensor_scalar(iwt[:].rearrange("p a b -> p (a b)"), bank[:, 0:32], 8.0 ** -0.5, None,
                                                ALU.mult), tp)
            pj.give(bi, t_iw)

            gs = Slots(G[0:4])
            acc = {}
            for i in (1, 2, 3):
                L = 128 * (i + 1)
                for e8 in range(8):
                    r = slice(64 * (e8 % 2), 64 * (e8 % 2) + 64)
                    gi, g, w = gs.take()
                    tp = PE(lambda e: e.matmul(g[:, 0:L], Q[r, e8 // 2, i * 128:(i + 1) * 128], ik[r, 0:L],
                                               start=True, stop=True), iq_tok, a1, t_ik, w)
                    i1, b1, w1 = tmp.take()
                    a = AC(lambda e: e.activation(b1[:, 0:L], g[:, 0:L], ACT.Relu, scale=0.125), tp, w1)
                    gs.give(gi, a)
                    if e8 == 0:
                        t = DV(lambda e: e.tensor_scalar(sel[i], b1[:, 0:L], iwt[:, i, 0:1], 0.0, ALU.mult, ALU.add),
                               a, t_iw)
                    else:
                        t = DV(lambda e: e.scalar_tensor_tensor(sel[i], b1[:, 0:L], iwt[:, i, e8:e8 + 1], sel[i],
                                                                ALU.mult, ALU.add), a, t)
                    tmp.give(i1, t)
                acc[i] = DV(lambda e: e.tensor_tensor(sel[i][:, L - 128:L], sel[i][:, L - 128:L], C("adm"), ALU.add), t)
            idx_done = tp
            g_free = [t_ for f in gs.free for t_ in f]

            t_mk = {0: DV(lambda e: e.tensor_scalar(MK[0], C("adm"), NEG, None, ALU.max))}
            todo = [(r, i) for r in range(16) for i in (1, 2, 3)]

            def top(n):
                for _ in range(min(n, len(todo))):
                    r, i = todo.pop(0)
                    t = DV(lambda e: e.max(m8[:, i - 1, :], sel[i]), acc[i])
                    acc[i] = DV(lambda e: e.match_replace(sel[i], m8[:, i - 1, :], sel[i], TAKEN), t)
                    if r == 15:
                        m = MK[i]
                        t = DV(lambda e: e.tensor_scalar(m, sel[i], -3.3e38, -1.0, ALU.is_le, ALU.add), acc[i])
                        t_mk[i] = DV(lambda e: e.tensor_scalar(m, m, -NEG, None, ALU.mult), t)

            bi, bank, tp = project((Hh, Hl), h_toks, 128)
            i1, b1, w1 = tmp.take()
            a = AC(lambda e: e.activation(b1, bank, ACT.Square), tp, w1)
            b2i, bank2, w = pj.take()
            m = PE(lambda e: e.matmul(bank2, ones[:], b1, start=True, stop=True), a, w)
            tr = rstd_of(bank2, m, b1, 128, EPS)
            pj.give(b2i, tr)
            t_cT = DV(lambda e: e.scalar_tensor_tensor(cT[:], bank, V("kv_g"), b1, ALU.mult, ALU.mult), tr)
            pj.give(bi, t_cT)
            tmp.give(i1, t_cT)
            bi, bank, tp = transposes(cT, t_cT)
            t_ct = AC(lambda e: e.activation(ctok[:].rearrange("p a r -> p (a r)"), bank, ACT.Copy), tp)
            pj.give(bi, t_ct)
            pump()

            def sigmoid(dst, bank, tp, w):
                a = AC(lambda e: e.activation(dst, bank, ACT.Exp, scale=-1.0), tp, w)
                x = DV(lambda e: e.tensor_scalar(dst, dst, 1e18, 1.0, ALU.min, ALU.add), a)
                a = AC(lambda e: e.activation(dst, dst, ACT.Ln), x)
                return AC(lambda e: e.activation(dst, dst, ACT.Exp, scale=-1.0), a)

            b_tok, k_tok, q_tok, v_tok = [], [], [], []
            for h in range(4):
                bi, bank, tp = project((Hh, Hl), h_toks, 128)
                i1, s1, w1 = tmp.take()
                a = sigmoid(s1, bank, tp, w1)
                pj.give(bi, a)
                x = DV(lambda e: e.tensor_scalar(s1, s1, oml[:, h:h + 1], lb[:, h:h + 1], ALU.mult, ALU.add), a, t_lb)
                k_tok.append(DV(lambda e: e.tensor_scalar(K[:, h, :], s1, -1.0, 1.0, ALU.mult, ALU.add), x))
                i2, s2, w2 = tmp.take()
                a = AC(lambda e: e.activation(s2, s1, ACT.Ln), x, w2)
                tmp.give(i1, a, k_tok[-1])
                b_tok.append(DV(lambda e: e.tensor_tensor_scan(Bc[:, h, :], C("scan"), s2, 0.0, ALU.mult, ALU.add), a))
                tmp.give(i2, b_tok[-1])
                pump()
                top(4)
            for h in range(4):
                bi, bank, tp = project((Hh, Hl), h_toks, 128)
                i1, s1, w1 = tmp.take()
                a = sigmoid(s1, bank, tp, w1)
                q_tok.append(DV(lambda e: e.tensor_tensor(Q[:, h, :], bank, s1, ALU.mult), a, idx_done))
                pj.give(bi, q_tok[-1])
                tmp.give(i1, q_tok[-1])
                pump()
                top(4)
            for h in range(4):
                bi, bank, tp = project((Hh, Hl), h_toks, 128)
                i1, a1_, w1 = tmp.take()
                a = AC(lambda e: e.activation(a1_, bank, ACT.Copy), tp, w1)
                pj.give(bi, a)
                bi, bank, tp = transposes(a1_, a)
                tmp.give(i1, tp)
                a = AC(lambda e: e.activation(vT[:, :, h * 128:(h + 1) * 128], bank.rearrange("p (a b) -> p a b", a=4),
                                              ACT.Copy), tp)
                pj.give(bi, a)
                v_tok.append(a)
                pump()
                top(4)

            t_sh = PO(lambda e: e.memset(SH[:], 0.0), t_rb, t_scr)
            SHv = SH[:].rearrange("p a b -> p (a b)").rearrange("p (q t h s) -> p q t h s", q=2, t=4, h=2)
            fb_free = [[t_ik, tp, idx_done], [t_ik, idx_done]]
            sh_tok = [[t_sh], [t_sh]]
            gs = Slots(G)
            for i in range(5):
                gs.give(i, *g_free)
            for lv, half in enumerate(LEVELS + (0,)):
                mask = con[:, CON["lev"][0] + lv * 128:CON["lev"][0] + (lv + 1) * 128].bitcast(U32)
                for q in range(2):
                    src = lambda x: x[:, 2 * q:2 * q + 2, :]
                    two = lambda x: x.rearrange("p h t -> p (h t)").rearrange("p (n a c) -> p n a c", a=2, c=half)
                    if half:
                        Fv, Bv, Kv, Qv = two(src(FB)), two(src(Bc)), two(src(K)), two(src(Q))
                        nb = 512 // half
                        ref = src(Bc).rearrange("p h t -> p (h t)").rearrange("p (n c) -> p n c", c=2 * half)[
                            :, :, half - 1:half].to_broadcast([P, nb, 2 * half])
                        full = lambda x: src(x).rearrange("p h t -> p (h t)").rearrange("p (n c) -> p n c", c=2 * half)
                        d = DV(lambda e: e.tensor_tensor(full(FB), full(Bc), ref, ALU.subtract), b_tok, fb_free[q])
                        e1 = AC(lambda e: e.activation(Fv[:, :, 0], Fv[:, :, 0], ACT.Exp, scale=-1.0), d)
                        e2 = AC(lambda e: e.activation(Fv[:, :, 1], Fv[:, :, 1], ACT.Exp), d)
                        x1 = PO(lambda e: e.tensor_tensor(Fv[:, :, 0], Fv[:, :, 0], Kv[:, :, 0], ALU.mult), e1, k_tok)
                        x2 = DV(lambda e: e.tensor_tensor(Fv[:, :, 1], Fv[:, :, 1], Qv[:, :, 1], ALU.mult), e2, q_tok)
                        left = right = FB
                        have = [x1, x2]
                    else:
                        left, right, have = K, Q, [k_tok, q_tok]
                    for tt in range(0, 4, 2):
                        gi, g, w = gs.take()
                        for n in range(4):
                            t_, h = tt + n // 2, 2 * q + n % 2
                            ts_ = slice(t_ * 128, (t_ + 1) * 128)
                            tp = PE(lambda e: e.matmul(g[:, n * 128:(n + 1) * 128], left[:, h, ts_], right[:, h, ts_],
                                                       start=True, stop=True), have, w, inc=n == 3)
                        dst = SHv[:, q, tt:tt + 2].rearrange("p t h s -> p (t h) s")
                        x = DV(lambda e: e.copy_predicated(dst, mask.unsqueeze(1).to_broadcast([P, 4, 128]),
                                                           g.rearrange("p (a s) -> p a s", a=4)), tp, sh_tok[q])
                        gs.give(gi, x)
                        sh_tok[q].append(x)
                    if half:
                        fb_free[q] = [tp]
                top(100 if lv > 4 else 2)
            score_tok = [sh_tok, t_sh]

            qx, ks = [], []
            for h in range(4):
                a = AC(lambda e: e.activation(FB[:, h, :], Bc[:, h, :], ACT.Exp), fb_free[h // 2], b_tok)
                d = DV(lambda e: e.tensor_copy(dec[:, h, :], FB[:, h, :].rearrange("p (n c) -> p n c", c=64)[:, :, 63]), a)
                qx.append(DV(lambda e: e.tensor_tensor(FB[:, h, :], FB[:, h, :], Q[:, h, :], ALU.mult), d, q_tok))
                i1, b1, w1 = tmp.take()
                b3 = Bc[:, h, :].rearrange("p (n c) -> p n c", c=64)
                t = DV(lambda e: e.tensor_tensor(b1.rearrange("p (n c) -> p n c", c=64), b3,
                                                 b3[:, :, 63:64].to_broadcast([P, 8, 64]), ALU.subtract), b_tok, w1)
                a = AC(lambda e: e.activation(b1, b1, ACT.Exp, scale=-1.0), t)
                t = DV(lambda e: e.tensor_tensor(b1, b1, K[:, h, :], ALU.mult), a, k_tok)
                bi, bank, tp = transposes(b1, t)
                tmp.give(i1, tp)
                a = AC(lambda e: e.activation(ksT[:, :, h * 128:(h + 1) * 128], bank.rearrange("p (a b) -> p a b", a=4),
                                              ACT.Copy), tp)
                pj.give(bi, a)
                ks.append(a)
            b_done = [DV.now(), AC.now()]

            def finish(t, ob, tp):
                i1, sq, w1 = tmp.take()
                a = AC(lambda e: e.activation(sq, ob[0], ACT.Square), tp, w1)
                bi, bank, w = pj.take()
                m = PE(lambda e: e.matmul(bank, ones[:], sq, start=True, stop=True), a, w)
                tr = rstd_of(bank, m, sq, 128, EPS)
                pj.give(bi, tr)
                for h in range(4):
                    x = DV(lambda e: e.scalar_tensor_tensor(Q[:, h, t * 128:(t + 1) * 128], ob[0][:, h * 128:(h + 1) * 128],
                                                            V("hg_g", h), sq[:, h * 128:(h + 1) * 128], ALU.mult, ALU.mult),
                           tr, qx)
                tmp.give(i1, x)
                ob_tok.append(x)
                return x

            ob_tok = []
            S = Bc[:].rearrange("p a b -> p (a b)")[:, 0:1536].rearrange("p (s h v) -> p s h v", s=3, h=4)
            SHt = lambda t: SHv[:, :, t].rearrange("p q h s -> p q h s")

            class Heads:
                def __init__(self, t):
                    self.t = t

                def __getitem__(self, ix):
                    return SHv[:, ix[1] // 2, self.t, ix[1] % 2, :]

            ksv = ksT[:].rearrange("p t (h k) -> p t h k", h=4)
            linear_attention(S, b_done, 4, 1, FB, qx, lambda t: (Heads(t), score_tok), ksv, ks, vT, v_tok, dec, qx, finish)
            core_done = [PE.now(), AC.now(), DV.now()]

            TB = SH
            t_tb = {}
            for h in range(4):
                ap = scr[h]
                skew = bass.AP(tensor=ap.tensor, offset=ap.offset + 127, ap=[[639, 128], [1, 512]])
                t_tb[h] = SP.dma(lambda e: e.dma_start(TB[:, h, :], skew), cnt(f"tb{h}"), core_done, t_scr)
            wk = Slots([ksT[:, i, :] for i in range(4)] + [FB[:, i, :] for i in range(4)])
            for i in range(8):
                wk.give(i, *core_done)
            gs = Slots(G[0:4])
            for i in range(4):
                gs.give(i, *core_done)
            QL = K
            o_toks, o_free = [], [None]
            SCALE = 128.0 ** -0.5
            for h in range(4):
                bi, bank, tp = project((Hh, Hl), h_toks, 128)
                i1, qa, w1 = wk.take()
                a = AC(lambda e: e.activation(qa, bank, ACT.Copy), tp, w1)
                pj.give(bi, a)
                pump()
                bi, bank, w = pj.take()
                tp = PE(lambda e: e.matmul(bank, wuk[:, h, :], qa, start=True, stop=True), a, t_uk, w)
                wk.give(i1, tp)
                t_ql = AC(lambda e: e.activation(QL[:, h, :], bank, ACT.Copy), tp, core_done)
                pj.give(bi, t_ql)
                turn = {}
                for i in range(4):
                    L = 128 * (i + 1)
                    sl = st[:, i, :]
                    gi, g, w = gs.take()
                    tp = PE(lambda e: e.matmul(g[:, 0:L], QL[:, h, i * 128:(i + 1) * 128], cT[:, 0:L], start=True, stop=True),
                            t_ql, t_cT, w)
                    pi, p, w = wk.take()
                    t = DV(lambda e: e.scalar_tensor_tensor(p[:, 0:L], g[:, 0:L], SCALE, TB[:, h, 384 - 128 * i:512],
                                                            ALU.mult, ALU.add), tp, w, t_tb[h])
                    gs.give(gi, t)
                    t = DV(lambda e: e.tensor_tensor(p[:, 0:L], p[:, 0:L], MK[i], ALU.add), t, t_mk[i])
                    t = DV(lambda e: e.reduce_max(sl[:, 0:1], p[:, 0:L], axis=AX.X, negate=True), t)
                    t = AC(lambda e: e.activation(p[:, 0:L], p[:, 0:L], ACT.Exp, bias=sl[:, 0:1], accum_out=sl[:, 1:2]), t)
                    t2 = DV(lambda e: e.reciprocal(sl[:, 2:3], sl[:, 1:2]), t)
                    t = DV(lambda e: e.tensor_scalar(p[:, 0:L], p[:, 0:L], sl[:, 2:3], None, ALU.mult), t2)
                    turn[i] = (pi, p, t)
                bi, bank, tp = project((Hh, Hl), h_toks, 128)
                i3, sg, w3 = tmp.take()
                a = sigmoid(sg, bank, tp, w3)
                t_sga = DV(lambda e: e.tensor_tensor(sg, bank, sg, ALU.mult), a)
                pj.give(bi, t_sga)
                pump()
                for i in range(4):
                    pi, p, t = turn[i]
                    bi, bank, w = pj.take()
                    for s in range(i + 1):
                        tp = PE(lambda e: e.transpose(bank[:, s * 128:(s + 1) * 128], p[:, s * 128:(s + 1) * 128], ident),
                                t, w, inc=s == i)
                    wk.give(pi, tp)
                    ai, aT, w = tmp.take()
                    a = AC(lambda e: e.activation(aT[:, 0:128 * (i + 1)], bank[:, 0:128 * (i + 1)], ACT.Copy), tp, w)
                    pj.give(bi, a)
                    for s in range(i + 1):
                        tp = PE(lambda e: e.matmul(G[4][:, i * 128:(i + 1) * 128], ctok[:, s, :],
                                                   aT[:, s * 128:(s + 1) * 128], start=s == 0, stop=s == i),
                                a, t_ct, o_free[0], core_done, inc=s == i)
                    tmp.give(ai, tp)
                i1, ol, w1 = tmp.take()
                a = AC(lambda e: e.activation(ol, G[4], ACT.Copy), tp, w1)
                o_free[0] = a
                bi, bank, w = pj.take()
                tp = PE(lambda e: e.matmul(bank, wuv[:, h, :], ol, start=True, stop=True), a, t_uv, w)
                tmp.give(i1, tp)
                t = DV(lambda e: e.tensor_tensor(sg, bank, sg, ALU.mult), tp, t_sga)
                pj.give(bi, t)
                both = split_out(sg, Oh[:, h, :], Ol[:, h, :], t, o_last)
                tmp.give(i3, *both)
                o_toks += both
                bi, bank, tp = project((Hh, Hl), h_toks, 128)
                i3, sg, w3 = tmp.take()
                a = sigmoid(sg, bank, tp, w3)
                t = DV(lambda e: e.tensor_tensor(sg, bank, sg, ALU.mult), a)
                pj.give(bi, t)
                t = DV(lambda e: e.tensor_tensor(sg, sg, Q[:, h, :], ALU.mult), t, ob_tok)
                both = split_out(sg, Oh[:, 4 + h, :], Ol[:, 4 + h, :], t, o_last)
                tmp.give(i3, *both)
                o_toks += both
                pump()

            for j in range(8):
                bi, bank, tp = project((Oh, Ol), [o_toks] * 8, 128)
                t = DV(lambda e: e.scalar_tensor_tensor(X[:, j, :], X[:, j, :], ALPHA, bank, ALU.mult, ALU.add), tp)
                pj.give(bi, t)
                if j == 0:
                    s = PO(lambda e: e.tensor_copy(SSQ[:], X[:, 0, :]), t, ssq_free)
                else:
                    s = PO(lambda e: e.tensor_tensor(SSQ[:], SSQ[:], X[:, j, :], ALU.add), t, s)
                pump()
            bi, bank, w = pj.take()
            tp = PE(lambda e: e.matmul(bank, ones[:], SSQ[:], start=True, stop=True), s, w)
            ssq_free[0] = tp
            for j in range(8):
                t = DV(lambda e: e.scalar_tensor_tensor(X[:, j, :], bank, -1.0 / 1024, X[:, j, :], ALU.mult, ALU.add), tp)
                s = ssq_add(j, t)
            pj.give(bi, t)
            bi, bank, w = pj.take()
            tp = PE(lambda e: e.matmul(bank, ones[:], SSQ[:], start=True, stop=True), s, w)
            a = AC(lambda e: e.activation(RS[:], bank, ACT.Ln, scale=1.0 / 1024, bias=epsb[:, 1:2]), tp)
            tr = AC(lambda e: e.activation(RS[:], RS[:], ACT.Exp, scale=-0.5), a)
            for j in range(8):
                t = DV(lambda e: e.scalar_tensor_tensor(X[:, j, :], X[:, j, :], V("ln_g", j), RS[:], ALU.mult, ALU.mult), tr)
                t = AC(lambda e: e.activation(X[:, j, :], X[:, j, :], ACT.Identity, bias=V("ln_b", j)), t)
                SP.dma(lambda e: e.dma_start(out[:, j, :], X[:, j, :]), cnt("out"), t)
        SP.wait((counters["out"][0], counters["out"][1]))


def shape_constants():
    con = np.zeros((P, NCON), np.float32)

    def put(name, a):
        o, n = CON[name]
        con[:, o:o + n] = a

    s, t = np.arange(P)[:, None], np.arange(P)[None, :]
    put("ident", (s == t))
    put("tri", (s // 64 == t // 64) & (s <= t))
    put("scan", np.broadcast_to((np.arange(T) % 64 != 0).astype(np.float32), (P, T)))
    lev = [(s // (2 * h) == t // (2 * h)) & (s // h % 2 == 0) & (t // h % 2 == 1) for h in LEVELS] + [s == t]
    put("lev", np.concatenate(lev, axis=1))
    rot = np.zeros((P, P), np.float32)
    for b in (0, 64):
        for i in range(8):
            rot[b + 8 + i, b + i] = -1.0
            rot[b + i, b + 8 + i] = 1.0
    put("rot", rot)
    put("adm", np.where(t // 64 <= s // 64, 0.0, FILL))
    put("cau", np.where(t <= s, 0.0, NEG))
    inv = (np.float32(500000.0) ** (-np.arange(0, 16, 2, dtype=np.float32) / np.float32(16))).astype(np.float32)
    p = np.arange(P) % 64
    put("freq", np.where(p < 16, inv[p % 8], 0.0).astype(np.float32)[:, None])
    rel = np.arange(640) - 511
    n = np.abs(rel)
    nf = np.maximum(n, 1).astype(np.float32)
    large = 8 + (np.log(nf / np.float32(8)) / np.float32(math.log(32.0)) * np.float32(8)).astype(np.int32)
    buck = np.where(rel > 0, 16, 0) + np.where(n < 8, n, np.minimum(large, 15))
    hot = (np.arange(32)[:, None] == buck[None, :]).astype(np.float32)
    return con, hot


def tiles(w, cols=128):
    w = np.ascontiguousarray(w)
    n = w.shape[1] // cols
    return np.ascontiguousarray(w.reshape(8, P, n, cols).transpose(2, 1, 0, 3)).reshape(n, P, 8 * cols)


def layout(i):
    col = lambda v: np.ascontiguousarray(v).reshape(-1, P).T
    a = {k: np.asarray(v) for k, v in i.items()}
    con, hot = shape_constants()
    parts = [a["c"], a["norm_g"][0, 0], a["norm_g"][0, 1], a["norm_g"][1, 0], a["norm_g"][1, 1], a["final_g"],
             a["ada_b"], a["gla_b_a"], a["gla_b_r"], a["gla_norm_g"], a["diff_subln_g"], a["kv_norm_g_2"],
             a["hgrn_norm_g_2"], a["lb_logits_2"], a["ln_g_2"], a["ln_b_2"]]
    d = {"con": con, "hot": hot, "vec": np.ascontiguousarray(np.concatenate([col(v) for v in parts], axis=1))}
    d["xT"] = np.ascontiguousarray(a["x"][0].T)
    d["pos"] = np.ascontiguousarray(a["positions"])
    d["ada"] = np.ascontiguousarray(a["ada_w"].reshape(2, 4, 2, P, 12, T).transpose(0, 4, 1, 3, 2, 5)).reshape(2, 12, 4, P, 2 * T)
    g = a["gla_w_in"][0]
    d["gla_in"] = tiles(g[:, :3072])
    d["w_a"] = tiles(g[:, 3072:], 16)[0]
    d["w_a2"] = np.ascontiguousarray(a["gla_w_a2"][0])
    d["gla_wo"] = tiles(a["gla_w_o"][0])
    for l in range(2):
        d[f"w1_{l}"] = tiles(a["mlp_w1"][l])
        d[f"w2_{l}"] = np.concatenate([tiles(a["mlp_w2"][l][r * 1024:(r + 1) * 1024]) for r in range(4)])
    d["diff_in"] = tiles(a["diff_w_in"][0])
    d["diff_wo"] = tiles(a["diff_w_o"][0])
    d["lam"] = np.ascontiguousarray(a["diff_lambda"][0].reshape(1, 256))
    w = a["w_in_2"][0]
    d["in_q"] = tiles(w[:, 0:512])
    d["in_c"] = tiles(w[:, 512:640])
    d["in_iq"] = tiles(w[:, 640:1152])
    d["in_ik"] = tiles(w[:, 1152:1224], 72)[0]
    d["in_ag"] = tiles(w[:, 1224:1736])
    d["in_b"] = tiles(w[:, 1736:3784])
    d["w_uk"] = np.ascontiguousarray(a["w_uk_2"][0].transpose(1, 0, 2)).reshape(P, 512)
    d["w_uv"] = np.ascontiguousarray(a["w_uv_2"][0].transpose(1, 0, 2)).reshape(P, 512)
    d["rel"] = np.ascontiguousarray(a["rel_bias_2"])
    d["wo_2"] = tiles(a["w_o_2"][0])
    return d


def kernel(**inputs):
    import concourse.bacc as bacc
    from concourse.bass_utils import run_bass_kernel_spmd

    nc = bacc.Bacc("TRN2", target_bir_lowering=False, num_devices=1, dynamic_dma_scratch_size=2048)
    arrays = layout(inputs)
    D = {k: nc.dram_tensor(k, v.shape, mybir.dt.from_np(v.dtype), kind="ExternalInput").ap() for k, v in arrays.items()}
    out = nc.dram_tensor("yT", (P, 8, T), F, kind="ExternalOutput").ap()
    build(nc, D, out)
    r = run_bass_kernel_spmd(nc, [arrays], core_ids=[0])
    y = r.results[0]["yT"]
    return np.ascontiguousarray(y.transpose(2, 1, 0)).reshape(1, T, 1024)
```

```python
import math
from contextlib import ExitStack

import numpy as np

import concourse.bass as bass
from concourse import mybir

F = mybir.dt.float32
R = mybir.dt.float32r
B16 = mybir.dt.bfloat16
I32 = mybir.dt.int32
U32 = mybir.dt.uint32
ALU = mybir.AluOpType
ACT = mybir.ActivationFunctionType
AX = mybir.AxisListType
P = 128
T = 512
EPS = 1e-6
LN_EPS = 1e-5
LAMBDA_INIT = 0.8 - 0.6 * math.exp(-0.3)
ALPHA = 2.0 ** 0.25
NEG = -1e30
FILL = -3.0e38
TAKEN = -3.4028234663852886e38
TWO_PI = 2.0 * math.pi
C1 = 6.28125
C2 = float(np.float32(int((TWO_PI - C1) * 2 ** 22) / 2.0 ** 22))
C3 = TWO_PI - C1 - C2

VEC = {"c": (0, 8), "n00": (8, 8), "n01": (16, 8), "n10": (24, 8), "n11": (32, 8), "fin": (40, 8),
       "ada_b": (48, 96), "b_a": (144, 4), "b_r": (148, 8), "gla_g": (156, 2), "sub_g": (158, 1),
       "kv_g": (159, 1), "hg_g": (160, 4), "lb": (164, 8), "ln_g": (172, 8), "ln_b": (180, 8)}
NVEC = 188
CON = {"ident": (0, 128), "tri": (128, 128), "scan": (256, 512), "lev": (768, 7 * 128),
       "rot": (1664, 128), "adm": (1792, 128), "cau": (1920, 128), "freq": (2048, 1), "ropem": (2049, 1)}
NCON = 2050
LEVELS = (32, 16, 8, 4, 2, 1)


class Queue:

    def __init__(self, eng, sem):
        self.eng, self.sem, self.n, self.seen = eng, sem, 0, {}

    def wait(self, w):
        if w is None:
            return
        if isinstance(w, list):
            for x in w:
                self.wait(x)
            return
        s, v = w
        if v > self.seen.get(id(s), 0):
            self.eng.wait_ge(s, v)
            self.seen[id(s)] = v

    def __call__(self, fn, *waits, inc=True):
        for w in waits:
            self.wait(w)
        ins = fn(self.eng)
        if inc:
            ins.then_inc(self.sem, 1)
            self.n += 1
            return (self.sem, self.n)

    def dma(self, fn, counter, *waits):
        for w in waits:
            self.wait(w)
        counter[1] += 16
        fn(self.eng).then_inc(counter[0], 16)
        return (counter[0], counter[1])

    def now(self):
        return (self.sem, self.n)


class Slots:

    def __init__(self, bufs, *tokens):
        self.bufs, self.free = bufs, [(i, list(tokens)) for i in range(len(bufs))]

    def take(self):
        i, w = self.free.pop(0)
        return i, self.bufs[i], w

    def give(self, i, *tokens):
        self.free.append((i, list(tokens)))


def build(nc, D, out, debug=None):
    ctx = ExitStack()
    with ctx:
        def sb(name, shape, dt=F, c=ctx):
            return c.enter_context(nc.sbuf_tensor("sb_" + name, shape, dt))

        sem = lambda n: ctx.enter_context(nc.semaphore(n))
        SP, AC, DV, PO, PE = (Queue(e, sem(f"s_{n}")) for n, e in (
            ("sp", nc.sync), ("act", nc.scalar), ("dve", nc.vector), ("pool", nc.gpsimd), ("pe", nc.tensor)))
        counters = {}

        def cnt(name):
            if name not in counters:
                counters[name] = [sem("d_" + name), 0]
            return counters[name]

        X = sb("X", [P, 8, T])
        Hh, Hl = sb("Hh", [P, 8, T], R), sb("Hl", [P, 8, T], R)
        Oh, Ol = sb("Oh", [P, 8, T], R), sb("Ol", [P, 8, T], R)
        Wh, Wl = sb("Wh", [P, 3, 8, 128], R), sb("Wl", [P, 3, 8, 128], R)
        RAW = sb("RAW", [P, 3, 1024])
        vec = sb("vec", [P, NVEC])
        con = sb("con", [P, NCON])
        ones = sb("ones", [P, 128])
        identb = sb("identb", [P, 128], B16)
        caub = sb("caub", [P, 128], B16)
        MOD = sb("MOD", [P, 2, 48])
        SC = sb("SC", [P, 4, 8])
        cact = sb("cact", [P, 8])
        ctmp = sb("ctmp", [P, 16])
        nbr = sb("nbr", [P, 8])
        epsb = sb("epsb", [P, 2])
        ADA = sb("ADA", [P, 2, T])
        SSQ = sb("SSQ", [P, T])
        RS = sb("RS", [P, T])
        NT = 7
        TMP = sb("TMP", [P, NT, T])
        tmp = Slots([TMP[:, i, :] for i in range(NT)])
        PS = ctx.enter_context(nc.psum_tensor("PS", [P, 8, T], F))
        pj = Slots([PS[:, i, :] for i in range(2)])
        tb = Slots([PS[:, i, :] for i in (2, 3)])

        V = lambda n, j=0, k=1: vec[:, VEC[n][0] + j:VEC[n][0] + j + k]
        C = lambda n: con[:, CON[n][0]:CON[n][0] + CON[n][1]]
        ident = C("ident")
        four = lambda x: x.rearrange("p (a b) -> p a b", a=4)

        AC.eng.preload_act_table_set("natural_log_exp_and_others")
        t_vec = SP.dma(lambda e: e.dma_start(vec[:], D["vec"]), cnt("vec"))
        t_con = t_x = None

        raw = Slots([RAW[:, i, :] for i in range(3)])
        wsl = Slots([i for i in range(3)])

        def load(src, n=1024):
            i, buf, w = raw.take()
            t = SP.dma(lambda e: e.dma_start(buf[:, 0:n], src), cnt(f"raw{i}"), w)
            return i, buf, t

        plan, ready, tasks, fresh = [], [], [], []

        def pump():
            if plan and len(ready) < 3 and wsl.free:
                src, m = plan.pop(0)
                n = 8 * m
                ri, buf, t = load(src, n)
                si, _, w = wsl.take()
                view = buf[:, 0:n].rearrange("p (k m) -> p k m", k=8)
                a = AC(lambda e: e.activation(Wh[:, si, :, 0:m], view, ACT.Copy), t, w)
                b = DV(lambda e: e.tensor_tensor(Wl[:, si, :, 0:m], view, Wh[:, si, :, 0:m].bitcast(F), ALU.subtract), t, a, w)
                raw.give(ri, a, b)
                ready.append((si, m, a, b))

        def start(task):
            if next(task, 0) is None:
                fresh.append(task)

        def tick():
            for t in list(tasks):
                if next(t, 0) is not None:
                    tasks.remove(t)
            tasks.extend(fresh)
            fresh.clear()

        def flush():
            while tasks or fresh:
                tick()

        class Block:

            def __init__(self, rhs, m=128):
                self.si, bm, self.a, self.b = ready.pop(0)
                assert bm == m
                self.rhs, self.m = rhs, m
                self.bi, self.bank, self.w = pj.take()
                self.n = 0

            def add(self, k, toks):
                hi, lo = self.rhs
                for n, (ww, xx) in enumerate(((Wh, hi), (Wh, lo), (Wl, hi))):
                    t = PE(lambda e: e.matmul(self.bank[0:self.m, :], ww[:, self.si, k, 0:self.m], xx[:, k, :],
                                              start=self.n == 0 and n == 0, stop=self.n == 7 and n == 2),
                           self.w, self.a if n == 0 else None, self.b if n == 2 else None, toks, inc=self.n == 7 and n == 2)
                self.n += 1
                if self.n == 8:
                    wsl.give(self.si, t)
                    self.tp = t

        def project(rhs, toks, m=128):
            b = Block(rhs, m)
            for k in range(8):
                b.add(k, toks[k])
            return b.bi, b.bank, b.tp

        def projects(rhs, toks, n, evac, ks=8, ms=None, side=None, order=range(8)):
            two = [Block(rhs, (ms or {}).get(j, 128)) for j in range(2)]
            for k in order[:ks]:
                for b in two:
                    assert toks(k) is not None
                    b.add(k, toks(k))
                if ks < 8:
                    tick()
            if ks < 8:
                flush()
            for b in two:
                for k in order[ks:]:
                    b.add(k, toks(k))
            for j in range(n):
                if j < 2:
                    bi, bank, tp = two[j].bi, two[j].bank, two[j].tp
                else:
                    bi, bank, tp = project(rhs, [toks(k) for k in range(8)], (ms or {}).get(j, 128))
                evac(j, bi, bank, tp)
                tick()
                pump()
                if side:
                    side()

        t_neg = AC(lambda e: e.activation(ctmp[:, 0:8], V("c", 0, 8), ACT.Exp, scale=-1.0), t_vec)
        t = DV(lambda e: e.tensor_scalar(ctmp[:, 8:16], ctmp[:, 0:8], 1.0, None, ALU.add), t_neg)
        t = DV(lambda e: e.reciprocal(ctmp[:, 0:8], ctmp[:, 8:16]), t)
        t_c = DV(lambda e: e.tensor_tensor(cact[:], V("c", 0, 8), ctmp[:, 0:8], ALU.mult), t)
        t_nbr = DV(lambda e: e.tensor_scalar(nbr[:], V("b_r", 0, 8), -1.0, None, ALU.mult), t_vec)
        t_one = DV(lambda e: e.memset(ones[:], 1.0))
        t_eps = DV(lambda e: e.memset(epsb[:, 0:1], EPS))
        t_eps2 = DV(lambda e: e.memset(epsb[:, 1:2], LN_EPS))
        ada_state = {"step": 0, "free": [None, None], "tok": None}
        t_mod = {}

        def ada_sum(layer, g, acc, tok):
            yield
            bi, bank, w = tb.take()
            for c in range(4):
                tp = PE(lambda e: e.matmul(bank[:, c:c + 1], acc[:, c * 128:(c + 1) * 128], ones[:, 0:1],
                                           start=True, stop=True), tok, w, t_one, inc=c == 3)
            ada_state["free"][g % 2] = tp
            tm = DV(lambda e: e.tensor_tensor(MOD[:, layer, g * 4:g * 4 + 4], bank[:, 0:4],
                                              V("ada_b", layer * 48 + g * 4, 4), ALU.add), tp, t_vec)
            tb.give(bi, tm)
            t_mod[layer, g] = tm
            if g in (3, 9):
                which = 0 if g == 3 else 1
                t_mod[layer, "A", which] = DV(lambda e: e.scalar_tensor_tensor(
                    SC[:, layer * 2 + which, :], MOD[:, layer, g * 4 - 4:g * 4 + 4], 1.0, V(f"n{layer}{which}", 0, 8),
                    ALU.add, ALU.mult), tm, t_mod[layer, g - 1])

        def ada_step():
            s = ada_state["step"]
            if s >= 96:
                return
            ada_state["step"] += 1
            layer, g, part = s // 48, s % 48 // 4, s % 4
            ri, buf, t = load(D["ada"][layer, g, part])
            acc = ADA[:, g % 2, :]
            for j in range(2):
                k = part * 2 + j
                w = buf[:, j * T:(j + 1) * T]
                if k == 0:
                    tok = DV(lambda e: e.tensor_scalar(acc, w, cact[:, k:k + 1], None, ALU.mult),
                             t, t_c, ada_state["free"][g % 2])
                else:
                    tok = DV(lambda e: e.scalar_tensor_tensor(acc, w, cact[:, k:k + 1], acc, ALU.mult, ALU.add),
                             t, ada_state["tok"])
                ada_state["tok"] = tok
            raw.give(ri, tok)
            if part == 3:
                start(ada_sum(layer, g, acc, tok))

        ssq = {"free": None}

        def ssq_add(j, xtok):
            if j == 0:
                ssq["t"] = AC(lambda e: e.activation(SSQ[:], X[:, 0, :], ACT.Square), xtok, ssq["free"])
            elif j == 7:
                ssq["last"] = AC(lambda e: e.activation(RS[:], X[:, 7, :], ACT.Square), xtok, ssq["free"])
            else:
                i, buf, w = tmp.take()
                a = AC(lambda e: e.activation(buf, X[:, j, :], ACT.Square), xtok, w)
                ssq["t"] = PO(lambda e: e.tensor_tensor(SSQ[:], SSQ[:], buf, ALU.add), a, ssq["t"])
                tmp.give(i, ssq["t"])

        def ssq_sum():
            bi, bank, w = tb.take()
            PE(lambda e: e.matmul(bank, ones[:], SSQ[:], start=True, stop=False), ssq["t"], w, t_one, inc=False)
            return bi, bank, PE(lambda e: e.matmul(bank, ones[:], RS[:], start=False, stop=True), ssq["last"])

        def rstd_of(bank, tok, dst, n, eps, *waits):
            a = AC(lambda e: e.activation(dst, bank, ACT.Ln, scale=1.0 / n, bias=eps), tok, t_eps, t_eps2, *waits)
            return AC(lambda e: e.activation(dst, dst, ACT.Exp, scale=-0.5), a)

        def norm(h_free, A=None, Bc=None, ab=(), g=None):
            bi, bank, tp = ssq_sum()
            tr = rstd_of(bank, tp, RS[:], 1024, epsb[:, 0:1])
            tb.give(bi, tr)
            res = []
            pend = None

            def low(j, i2, src, x2, a):
                b = DV(lambda e: e.tensor_tensor(Hl[:, j, :], src, Hh[:, j, :].bitcast(F), ALU.subtract), x2, a, h_free)
                if i2 is not None:
                    tmp.give(i2, b)
                res.append([a, b])

            for j in range(8):
                if g is None:
                    eng = PO if j in (2, 4, 6) else DV
                    i, buf, w = tmp.take()
                    x1 = eng(lambda e: e.tensor_tensor(buf, X[:, j, :], RS[:], ALU.mult), tr, w, t_x)
                    a = AC(lambda e: e.activation(Hh[:, j, :], buf, ACT.Identity, scale=A[:, j:j + 1],
                                                  bias=Bc[:, j:j + 1]), x1, h_free, *ab)
                    i2, buf2, w2 = tmp.take()
                    x2 = DV(lambda e: e.tensor_scalar(buf2, buf, A[:, j:j + 1], Bc[:, j:j + 1], ALU.mult, ALU.add),
                            x1, w2, *ab)
                    tmp.give(i, a, x2)
                    if pend:
                        low(*pend)
                    pend = (j, i2, buf2, x2, a)
                else:
                    x1 = DV(lambda e: e.scalar_tensor_tensor(X[:, j, :], X[:, j, :], V(g, j), RS[:], ALU.mult,
                                                             ALU.mult), tr, t_vec)
                    a = AC(lambda e: e.activation(Hh[:, j, :], X[:, j, :], ACT.Copy), x1, h_free)
                    if pend:
                        low(*pend)
                    pend = (j, None, X[:, j, :], x1, a)
            low(*pend)
            ssq["free"] = [res[-1], tp, x1]
            return res

        def residual(gate, j, bi, bank, tp, g_tok, last):
            t = DV(lambda e: e.scalar_tensor_tensor(X[:, j, :], bank, gate[:, j:j + 1], X[:, j, :], ALU.mult, ALU.add),
                   tp, g_tok, t_x)
            pj.give(bi, t)
            if last:
                ssq_add(j, t)

        def split_out(src, hi, lo, src_tok, *waits):
            a = AC(lambda e: e.activation(hi, src, ACT.Copy), src_tok, *waits)
            b = DV(lambda e: e.tensor_tensor(lo, src, hi.bitcast(F), ALU.subtract), src_tok, a, *waits)
            return [a, b]

        def turned(bank, src, tok, w, n=4):
            for i in range(n):
                tp = PE(lambda e: e.transpose(bank[:, i * 128:(i + 1) * 128], src[:, i * 128:(i + 1) * 128], ident),
                        tok, w, t_con, inc=i == n - 1)
            return tp

        def by_tokens(dst, src, i, tok, toks, key, *waits):
            yield
            bi, bank, w = tb.take()
            tp = turned(bank, src, tok, w)
            tmp.give(i, tp)
            toks[key] = AC(lambda e: e.activation(dst, four(bank), ACT.Copy), tp, *waits)
            tb.give(bi, toks[key])

        def values(dst, bi, bank, tp, toks, key, *waits):
            i1, a1, w1 = tmp.take()
            a = AC(lambda e: e.activation(a1, bank, ACT.Copy), tp, w1)
            pj.give(bi, a)
            return by_tokens(dst, a1, i1, a, toks, key, *waits)

        def sigmoid(dst, bank, tp, w, bias=0.0):
            a = AC(lambda e: e.activation(dst, bank, ACT.Exp, scale=-1.0, bias=bias), tp, w)
            x = DV(lambda e: e.tensor_scalar(dst, dst, 1e18, 1.0, ALU.min, ALU.add), a)
            a = AC(lambda e: e.activation(dst, dst, ACT.Ln), x)
            return AC(lambda e: e.activation(dst, dst, ACT.Exp, scale=-1.0), a)

        def mlp(layer, h_toks):
            gate = MOD[:, layer, 40:48]
            o_last = [None]
            o_toks = [None] * 8

            def hidden(c, bi, bank, tp):
                i, r, w = tmp.take()
                a = AC(lambda e: e.activation(r, bank, ACT.Relu), tp, w)
                pj.give(bi, a)
                hi = AC(lambda e: e.activation(Oh[:, c, :], r, ACT.Square), a, o_last[0])
                i2, q, w2 = tmp.take()
                s = DV(lambda e: e.tensor_tensor(q, r, r, ALU.mult), a, w2)
                lo = DV(lambda e: e.tensor_tensor(Ol[:, c, :], q, Oh[:, c, :].bitcast(F), ALU.subtract), s, hi, o_last[0])
                tmp.give(i, hi, s)
                tmp.give(i2, lo)
                o_toks[c] = [hi, lo]
                o_last[1:] = [tp]

            for g in range(4):
                if g == 0:
                    projects((Hh, Hl), lambda k: h_toks[k], 8, hidden, side=ada_step)
                else:
                    for c in range(8):
                        hidden(c, *project((Hh, Hl), h_toks))
                        tick()
                        pump()
                        ada_step()
                h_last = o_last[1]
                for d in range(8):
                    bi, bank, tp = project((Oh, Ol), o_toks)
                    o_last[0] = tp
                    residual(gate, d, bi, bank, tp, [t_mod[layer, 10], t_mod[layer, 11]], g == 3)
                    tick()
                    pump()
                    ada_step()
            return h_last, o_last[0]

        def state_and_values(sc, sc_tok, ksT, ks_tok, vT, v_tok, qd, q_tok, dec, d_tok, S, s_free, gs, ob, o_free, nv, res):
            W = nv * 128
            per = T // W
            st = {}
            s_t = s_free
            for n0 in range(0, 7, 2 * per):
                ns = range(n0, min(n0 + 2 * per, 7))
                banks = [gs.take(), gs.take()]
                tp = [None, None]
                at = lambda n: banks[n % 2][1][:, (n - n0) // 2 * W:((n - n0) // 2 + 1) * W]
                for par in range(2):
                    lo = 64 * par
                    mine = [n for n in ns if n % 2 == par]
                    for n in mine:
                        tp[par] = PE(lambda e: e.matmul(at(n), ksT[lo:lo + 64, n // 2, :], vT[lo:lo + 64, n // 2, :],
                                                        start=True, stop=True),
                                     banks[par][2], ks_tok, v_tok, inc=n == mine[-1])
                for n in ns:
                    if n == 0:
                        s_t = DV(lambda e: e.tensor_copy(S[:, 0, :], at(n)), tp[0], s_t)
                    else:
                        s_t = DV(lambda e: e.scalar_tensor_tensor(S[:, n, :], S[:, n - 1, :], dec[:, n:n + 1], at(n),
                                                                  ALU.mult, ALU.add), tp[n % 2], s_t, d_tok, s_free)
                    st[n + 1] = s_t
                for x in banks:
                    gs.give(x[0], s_t)
                if n0 + 2 * per < 7:
                    yield
            yield
            for v in range(nv):
                for t in range(4):
                    dst = ob[v][:, t * 128:(t + 1) * 128]
                    jobs = [(dst, vT[:, t, v * 128:(v + 1) * 128], sc(t), [sc_tok, v_tok, o_free])]
                    for n in (2 * t, 2 * t + 1):
                        if n > 0:
                            u = 64 * (n % 2)
                            jobs.append((dst[:, u:u + 64], S[:, n - 1, v * 128:(v + 1) * 128],
                                         qd[:, n * 64:(n + 1) * 64], [st[n], q_tok]))
                    for m, (o, l, r, w) in enumerate(jobs):
                        tp = PE(lambda e: e.matmul(o, l, r, start=m == 0, stop=m == len(jobs) - 1),
                                w, inc=m == len(jobs) - 1)
            res["tp"] = tp

        plan.append((D["w_a"], 16))
        for h in range(4):
            plan += [(D["gla_in"][j], 128) for j in (8 + 2 * h, 9 + 2 * h, 16 + 2 * h, 17 + 2 * h, 4 + h, h)]
        plan += [(D["gla_wo"][j], 128) for j in range(8)]
        for g in range(4):
            plan += [(D["w1_0"][g * 8 + c], 128) for c in range(8)]
            plan += [(D["w2_0"][g * 8 + c], 128) for c in range(8)]
        for h in range(8):
            plan += [(D["diff_in"][j], 128) for j in (16 + h, h, 8 + h)]
        plan += [(D["diff_wo"][j], 128) for j in range(8)]
        for g in range(4):
            plan += [(D["w1_1"][g * 8 + c], 128) for c in range(8)]
            plan += [(D["w2_1"][g * 8 + c], 128) for c in range(8)]
        plan += [(D["in_iq"][j], 128) for j in range(4)] + [(D["in_ik"], 72), (D["in_c"][0], 128)]
        for h in range(4):
            plan += [(D["in_b"][j], 128) for j in (4 + h, h, 8 + h)]
        plan += [(D["in_q"][j], 128) for j in range(4)]
        plan += [(D[n][j], 128) for n, j in (("in_b", 12), ("in_b", 13), ("in_ag", 0), ("in_ag", 1), ("in_b", 14),
                                             ("in_ag", 2), ("in_b", 15), ("in_ag", 3))]
        plan += [(D["wo_2"][j], 128) for j in range(8)]

        for s in range(16):
            ada_step()
            if s == 1:
                t_x = SP.dma(lambda e: e.dma_start(X[:], D["xT"].rearrange("(c p) t -> p c t", p=P)), cnt("x"))
                for j in range(8):
                    ssq_add(j, t_x)
            if s == 3:
                t_con = SP.dma(lambda e: e.dma_start(con[:], D["con"]), cnt("con"))
            tick()
        for _ in range(3):
            pump()
        flush()
        t_idb = DV(lambda e: e.tensor_copy(identb[:], ident), t_con)
        t_cau = DV(lambda e: e.tensor_copy(caub[:], C("cau")), t_con)
        h_toks = norm(None, SC[:, 0, :], MOD[:, 0, 0:8], (t_mod[0, "A", 0], t_mod[0, 0], t_mod[0, 1]))

        if debug == 4:
            for j in range(8):
                t = DV(lambda e: e.tensor_tensor(X[:, j, :], Hh[:, j, :].bitcast(F), Hl[:, j, :].bitcast(F), ALU.add), *h_toks)
            SP.dma(lambda e: e.dma_start(out, X[:]), cnt("out"), t)
            SP.wait((counters["out"][0], counters["out"][1]))
            return
        with ExitStack() as ph:
            qd, ki, ksT, S = (sb(n, [P, 2, T], c=ph) for n in ("qd", "ki", "ksT", "sct"))
            vT, rg = sb("vT", [P, 2, 4, 256], c=ph), sb("rg", [P, 2, 2, T], c=ph)
            sct = S
            S = sb("S", [P, 7, 256], c=ph)
            EX = sb("EX", [P, 2, 3, T], c=ph)
            dec = sb("dec", [P, 4, 8], c=ph)
            al = sb("al", [16, T], c=ph)
            wa2 = sb("wa2", [16, T], c=ph)
            t_wa2 = SP.dma(lambda e: e.dma_start(wa2[:], D["w_a2"]), cnt("wa2"))
            gs = Slots([PS[:, i, :] for i in (4, 5)])
            ob = [PS[:, 6, :], PS[:, 7, :]]
            tri = C("tri").unsqueeze(1).to_broadcast([P, 4, 128])
            tk = {}
            core_free = [None, None]
            ex_free = [None, None]
            o_toks = [None] * 8

            def gates(h):
                zi, z, w = tb.take()
                tz = PE(lambda e: e.matmul(z, wa2[:, h * 128:(h + 1) * 128], al[:], start=True, stop=True), t_wa2, t_al, w)
                EB, EN, EK = (EX[:, h % 2, i, :] for i in range(3))
                i1, a1, w1 = tmp.take()
                i2, a2, w2 = tmp.take()
                ta = AC(lambda e: e.activation(a1, z, ACT.Abs, bias=V("b_a", h)), tz, w1, t_vec)
                tm = DV(lambda e: e.tensor_scalar(a2, z, V("b_a", h), 0.0, ALU.add, ALU.min), tz, ta, w2, t_vec)
                tb.give(zi, ta, tm)
                ta = AC(lambda e: e.activation(a1, a1, ACT.Exp, scale=-1.0), ta)
                ta = AC(lambda e: e.activation(a1, a1, ACT.Ln, bias=1.0), ta)
                yield
                tm = DV(lambda e: e.tensor_tensor(a2, a2, a1, ALU.subtract), tm, ta)
                tb_ = DV(lambda e: e.tensor_tensor_scan(a1, C("scan"), a2, 0.0, ALU.mult, ALU.add), tm, t_con)
                tB = AC(lambda e: e.activation(EB, a1, ACT.Exp, scale=1.0 / 16), tb_, ex_free[h % 2])
                tN = AC(lambda e: e.activation(EN, a1, ACT.Exp, scale=-1.0 / 16), tb_)
                a13 = a1.rearrange("p (n c) -> p n c", c=64)
                a23 = a2.rearrange("p (n c) -> p n c", c=64)
                td = DV(lambda e: e.tensor_tensor(a23, a13, a13[:, :, 63:64].to_broadcast([P, 8, 64]), ALU.subtract), tb_)
                tK = AC(lambda e: e.activation(EK, a2, ACT.Exp, scale=-1.0 / 16), td)
                tk["d", h] = DV(lambda e: e.tensor_copy(dec[:, h, :], EB.rearrange("p (n c) -> p n c", c=64)[:, :, 63]), tB)
                tmp.give(i1, tB, tN, td)
                tmp.give(i2, tK)
                tk["e", h] = (tB, tN, tK)

            def head(h):
                b = h % 2
                yield
                bi, bank, w = tb.take()
                for t in range(4):
                    ts = slice(t * 128, (t + 1) * 128)
                    tp = PE(lambda e: e.matmul(bank[:, ts], ki[:, b, ts], qd[:, b, ts], start=True, stop=True),
                            w, tk["k", h], tk["q", h], inc=t == 3)
                x = DV(lambda e: e.tensor_tensor(four(sct[:, b, :]), four(bank), tri, ALU.mult), tp, core_free[b])
                tb.give(bi, x)
                res = {}
                yield from state_and_values(
                    lambda t: sct[:, b, t * 128:(t + 1) * 128], x, four(ksT[:, b, :]), tk["s", h],
                    vT[:, b], [tk["v", h, 0], tk["v", h, 1]], qd[:, b, :], tk["q", h], dec[:, h, :], tk["d", h],
                    S, tk.get("S"), gs, ob, tk.get("O"), 2, res)
                tp = res["tp"]
                tk["S"] = tp
                i1, s1, w1 = tmp.take()
                i2, s2, w2 = tmp.take()
                a1 = AC(lambda e: e.activation(s1, ob[0], ACT.Square), tp, w1)
                a2 = AC(lambda e: e.activation(s2, ob[1], ACT.Square), tp, w2)
                s = PO(lambda e: e.tensor_tensor(s1, s1, s2, ALU.add), a1, a2)
                yield
                bi, bank, w = tb.take()
                m = PE(lambda e: e.matmul(bank, ones[:], s1, start=True, stop=True), s, w)
                tr = rstd_of(bank, m, s1, 256, epsb[:, 0:1])
                tb.give(bi, tr)
                i3, s3, w3 = tmp.take()
                on = [s2, s3]
                xs = [DV(lambda e, v=v: e.scalar_tensor_tensor(on[v], ob[v], V("gla_g", v), s1, ALU.mult, ALU.mult),
                         tr, s, w3, t_vec) for v in range(2)]
                tk["O"] = [xs[1], a2]
                xs = [DV(lambda e, v=v: e.tensor_tensor(on[v], on[v], rg[:, b, v, :], ALU.mult), xs[v], tk["r", h, v])
                      for v in range(2)]
                for v in range(2):
                    o_toks[2 * h + v] = split_out(on[v], Oh[:, 2 * h + v, :], Ol[:, 2 * h + v, :], xs[v])
                tmp.give(i1, xs[1])
                tmp.give(i2, *o_toks[2 * h])
                tmp.give(i3, *o_toks[2 * h + 1])
                core_free[b] = [tp, xs[1]]

            def evac(n, bi, bank, tp):
                if n == 0:
                    nonlocal_al["t"] = AC(lambda e: e.activation(al[:], bank[0:16, :], ACT.Copy), tp)
                    pj.give(bi, nonlocal_al["t"])
                    return
                h, j = divmod(n - 1, 6)
                b = h % 2
                free = core_free[b]
                if j < 2:
                    start(values(vT[:, b, :, j * 128:(j + 1) * 128], bi, bank, tp, tk, ("v", h, j), free))
                    if j == 1 and h == 0:
                        start(gates(0))
                elif j < 4:
                    v = j - 2
                    i1, a1, w1 = tmp.take()
                    a = sigmoid(a1, bank, tp, w1, bias=nbr[:, 2 * h + v:2 * h + v + 1])
                    x = DV(lambda e: e.scalar_tensor_tensor(rg[:, b, v, :], bank, V("b_r", 2 * h + v), a1,
                                                            ALU.add, ALU.mult), a, free, t_nbr)
                    pj.give(bi, x)
                    tmp.give(i1, x)
                    tk["r", h, v] = x
                elif j == 4:
                    tB, tN, tK = tk["e", h]
                    EB, EN, EK = (EX[:, b, i, :] for i in range(3))
                    i3, kst, w3 = tmp.take()
                    x1 = DV(lambda e: e.tensor_tensor(kst, bank, EK, ALU.mult), tp, tK, w3)
                    x2 = DV(lambda e: e.tensor_tensor(ki[:, b, :], bank, EN, ALU.mult), tN, free)
                    pj.give(bi, x2)
                    tk["k", h] = x2
                    start(by_tokens(four(ksT[:, b, :]), kst, i3, x1, tk, ("s", h), free))
                else:
                    tB = tk["e", h][0]
                    x3 = DV(lambda e: e.scalar_tensor_tensor(qd[:, b, :], bank, 128.0 ** -0.5, EX[:, b, 0, :], ALU.mult,
                                                             ALU.mult), tp, tB, free)
                    pj.give(bi, x3)
                    tk["q", h] = x3
                    ex_free[b] = [x3, tk["d", h]]
                    start(head(h))
                    if h < 3:
                        start(gates(h + 1))

            nonlocal_al = {}

            class Al:
                pass

            def run_gla():
                nonlocal t_al
                b0 = Block((Hh, Hl), 16)
                b1 = Block((Hh, Hl))
                for k in range(8):
                    b0.add(k, h_toks[k])
                    b1.add(k, h_toks[k])
                evac(0, b0.bi, b0.bank, b0.tp)
                t_al = nonlocal_al["t"]
                evac(1, b1.bi, b1.bank, b1.tp)
                pump()
                ada_step()
                pump()
                for n in range(2, 25):
                    bi, bank, tp = project((Hh, Hl), h_toks)
                    evac(n, bi, bank, tp)
                    tick()
                    pump()
                    ada_step()
                return tp

            t_al = None
            h_last = run_gla()

            def wo(o_toks, gate, g_tok, ks):
                last = {}

                def evac(j, bi, bank, tp):
                    residual(gate, j, bi, bank, tp, g_tok(), True)
                    last["t"] = tp
                projects((Oh, Ol), lambda k: o_toks[k], 8, evac, ks=ks, side=ada_step)
                return last["t"]

            o_last = wo(o_toks, MOD[:, 0, 16:24], lambda: [t_mod[0, 4], t_mod[0, 5]], 6)
            mix_done = [PE.now(), AC.now(), DV.now(), PO.now()]
        flush()
        if debug == 5:
            SP.dma(lambda e: e.dma_start(out, X[:]), cnt("out"), ssq["last"])
            SP.wait((counters["out"][0], counters["out"][1]))
            return
        h_toks = norm([h_last], SC[:, 1, :], MOD[:, 0, 24:32], (t_mod[0, "A", 1], t_mod[0, 6], t_mod[0, 7]))
        h_last, o_last = mlp(0, h_toks)
        while ada_state["step"] < 96:
            ada_step()
        flush()
        if debug == 1:
            SP.dma(lambda e: e.dma_start(out, X[:]), cnt("out"), ssq["last"])
            SP.wait((counters["out"][0], counters["out"][1]))
            return
        h_toks = norm([h_last], SC[:, 2, :], MOD[:, 1, 0:8], (t_mod[1, "A", 0], t_mod[1, 0], t_mod[1, 1]))
        with ExitStack() as ph:
            vT = sb("dvT", [P, 3, 4, 128], c=ph)
            RC, RSn = sb("ropec", [P, T], c=ph), sb("ropes", [P, T], c=ph)
            QK = sb("QK", [P, 2, 2, T], c=ph)
            WK = sb("WK", [P, 14, T], c=ph)
            st = sb("st", [P, 8, 8], c=ph)
            lamb = sb("lamb", [P, 256], c=ph)
            lam2 = sb("lam2", [P, 8], c=ph)
            posi = sb("posi", [P, T], I32, c=ph)
            t_pos = SP.dma(lambda e: e.dma_start(posi[:], D["pos"].to_broadcast([P, T])), cnt("pos"), mix_done)
            t_lam = SP.dma(lambda e: e.dma_start(lamb[:], D["lam"].to_broadcast([P, 256])), cnt("lam"), mix_done)
            for q in (AC, DV, PO, PE):
                q.wait(mix_done)
            wk = Slots([WK[:, i, :] for i in range(14)])

            l4 = lamb[:].rearrange("p (a b d) -> p a b d", a=2, b=2)
            t = DV(lambda e: e.tensor_tensor(l4[:, :, 0, :], l4[:, :, 0, :], l4[:, :, 1, :], ALU.mult), t_lam)
            t = DV(lambda e: e.reduce_sum(lam2[:, 0:2], l4[:, :, 0, :], axis=AX.X), t)
            t = AC(lambda e: e.activation(lam2[:, 2:4], lam2[:, 0:2], ACT.Exp), t)
            t = DV(lambda e: e.tensor_tensor(lam2[:, 4:5], lam2[:, 3:4], lam2[:, 2:3], ALU.subtract), t)
            t_nl = DV(lambda e: e.tensor_scalar(lam2[:, 5:6], lam2[:, 4:5], -LAMBDA_INIT, None, ALU.add), t)
            nlam = lam2[:, 5:6]
            t_sg = DV(lambda e: e.tensor_scalar(lam2[:, 6:7], V("sub_g"), 1.0 - LAMBDA_INIT, None, ALU.mult))
            subg = lam2[:, 6:7]

            (i1, ang, w1), (i2, nn, w2) = wk.take(), wk.take()
            t = DV(lambda e: e.tensor_copy(ang, posi[:]), t_pos)
            t = DV(lambda e: e.tensor_scalar(ang, ang, C("freq"), None, ALU.mult), t)
            t = DV(lambda e: e.tensor_scalar(nn, ang, 1.0 / TWO_PI, 12582912.0, ALU.mult, ALU.add), t)
            t = DV(lambda e: e.tensor_scalar(nn, nn, -12582912.0, None, ALU.add), t)
            for c in (C1, C2, C3):
                t = DV(lambda e, c=c: e.scalar_tensor_tensor(ang, nn, -c, ang, ALU.mult, ALU.add), t)
            t = DV(lambda e: e.tensor_scalar(ang, ang, 3.1415925, -3.1415925, ALU.min, ALU.max), t)
            ts = AC(lambda e: e.activation(RSn[:], ang, ACT.Sin), t)
            t = DV(lambda e: e.scalar_tensor_tensor(nn, ang, -1.0, ang, ALU.mult, ALU.max), t)
            t = DV(lambda e: e.tensor_scalar(nn, nn, -1.0, math.pi / 2, ALU.mult, ALU.add), t)
            tc = AC(lambda e: e.activation(RC[:], nn, ACT.Sin), t)
            t_rope = [ts, tc]
            wk.give(i1, ts, t)
            wk.give(i2, tc)
            AC.eng.preload_act_table_set("natural_log_exp_and_others")

            tk = {}
            free = [None, None]
            g3 = PS[:, 4:7, :]
            g_free = [None] * 3
            ob = PS[:, 7, :]
            o_free = [None]
            o_toks = [None] * 8

            def rope(dst, bi, bank, tp, scale, h, key):
                i1, q, w1 = wk.take()
                a = AC(lambda e: e.activation(q, bank, ACT.Copy, scale=scale), tp, w1)
                pj.give(bi, a)
                i2, q2, w2 = wk.take()
                x1 = PO(lambda e: e.tensor_tensor(q2, q, RC[:], ALU.mult), a, t_rope, w2)
                yield
                bi, bank, w = tb.take()
                tr = PE(lambda e: e.matmul(bank, C("rot"), q, start=True, stop=True), a, w, t_con)
                wk.give(i1, tr, x1)
                i3, q3, w3 = wk.take()
                x2 = DV(lambda e: e.tensor_tensor(q3, bank, RSn[:], ALU.mult), tr, t_rope, w3)
                tb.give(bi, x2)
                tk[key, h] = DV(lambda e: e.tensor_tensor(dst, q2, q3, ALU.add), x1, x2, free[h % 2])
                wk.give(i2, tk[key, h])
                wk.give(i3, tk[key, h])

            def scores(h, i, at, w, both, one_bank):
                L = 128 * (i + 1)
                b = h % 2
                sl = st[:, (h * 4 + i) % 8, :]
                tp = None
                for m in range(2):
                    g = at(m)
                    r = slice(64 * m, 64 * m + 64)
                    PE(lambda e: e.matmul(g, QK[r, b, 0, i * 128:(i + 1) * 128], QK[r, b, 1, 0:L],
                                          start=True, stop=False), tk["q", h], tk["k", h], w, tp if one_bank else None, inc=False)
                    tp = PE(lambda e: e.matmul(g[:, L - 128:L], identb[:], caub[:], start=False, stop=True), t_idb, t_cau)
                tm = DV(lambda e: e.tensor_reduce(sl[:, 0:2], both, AX.X, ALU.max, negate=True), tp)
                ps, ex = [], []
                for m in range(2):
                    pi, p, wp = wk.take()
                    ps.append((pi, p))
                    ex.append(AC(lambda e: e.activation(p[:, 0:L], at(m), ACT.Exp, bias=sl[:, m:m + 1],
                                                        accum_out=sl[:, 2 + m:3 + m]), tm, wp))
                t = DV(lambda e: e.reciprocal(sl[:, 4:6], sl[:, 2:4]), ex[0], ex[1])
                t2 = DV(lambda e: e.tensor_tensor(sl[:, 6:7], sl[:, 5:6], nlam, ALU.mult), t, t_nl)
                p0, p1 = ps[0][1], ps[1][1]
                t = DV(lambda e: e.tensor_scalar(p0[:, 0:L], p0[:, 0:L], sl[:, 4:5], None, ALU.mult), t)
                t = DV(lambda e: e.scalar_tensor_tensor(p1[:, 0:L], p1[:, 0:L], sl[:, 6:7], p0[:, 0:L], ALU.mult, ALU.add),
                       t, t2)
                wk.give(ps[0][0], t)
                tk["p", h, i] = (ps[1][0], p1, t)
                return ex[1]

            def wide(h, i):
                L = 128 * (i + 1)
                x = scores(h, i, lambda m: g3[:, m, 0:L], [g_free[0], g_free[1]], g3[:, 0:2, 0:L], False)
                g_free[0:2] = [x, x]

            def narrow(h, i):
                L = 128 * (i + 1)
                x = scores(h, i, lambda m: g3[:, 2, 256 * m:256 * m + L], g_free[2],
                           g3[:, 2, :].rearrange("p (m l) -> p m l", m=2)[:, :, 0:L], True)
                g_free[2] = x

            def turn(h, i):
                pi, p, t = tk.pop(("p", h, i))
                bi, bank, w = tb.take()
                tp = turned(bank, p, t, w, i + 1)
                wk.give(pi, tp)
                ai, aT, w = wk.take()
                a = AC(lambda e: e.activation(aT[:, 0:128 * (i + 1)], bank[:, 0:128 * (i + 1)], ACT.Copy), tp, w)
                tb.give(bi, a)
                tk["T", h, i] = (ai, aT, a)

            def weigh(h, i):
                ai, aT, a = tk.pop(("T", h, i))
                for s in range(i + 1):
                    tp = PE(lambda e: e.matmul(ob[:, i * 128:(i + 1) * 128], vT[:, h % 3, s, :],
                                               aT[:, s * 128:(s + 1) * 128], start=s == 0, stop=s == i),
                            a, tk["v", h], o_free[0], inc=s == i)
                wk.give(ai, tp)
                return tp

            def attention(h):
                yield
                wide(h, 3)
                narrow(h, 0)
                yield
                turn(h, 0)
                wide(h, 2)
                yield
                turn(h, 3)
                narrow(h, 1)
                free[h % 2] = [PE.now()]
                yield
                turn(h, 2)
                weigh(h, 0)
                weigh(h, 3)
                yield
                turn(h, 1)
                weigh(h, 2)
                yield
                tp = weigh(h, 1)
                tk["done", h] = tp
                i1, sq, w1 = wk.take()
                i2, on, w2 = wk.take()
                x = AC(lambda e: e.activation(on, ob, ACT.Copy), tp, w2)
                o_free[0] = x
                a = AC(lambda e: e.activation(sq, on, ACT.Square), x, w1)
                yield
                bi, bank, w = tb.take()
                m = PE(lambda e: e.matmul(bank, ones[:], sq, start=True, stop=True), a, w)
                tr = rstd_of(bank, m, sq, 128, epsb[:, 0:1])
                tb.give(bi, tr)
                x = DV(lambda e: e.scalar_tensor_tensor(on, on, subg, sq, ALU.mult, ALU.mult), tr, t_sg)
                wk.give(i1, x)
                o_toks[h] = split_out(on, Oh[:, h, :], Ol[:, h, :], x, o_last)
                wk.give(i2, *o_toks[h])

            def evac(n, bi, bank, tp):
                h, j = divmod(n, 3)
                if j == 0:
                    start(values(vT[:, h % 3], bi, bank, tp, tk, ("v", h), tk.get(("done", h - 3))))
                elif j == 1:
                    start(rope(QK[:, h % 2, 0, :], bi, bank, tp, 0.125, h, "q"))
                else:
                    start(rope(QK[:, h % 2, 1, :], bi, bank, tp, 1.0, h, "k"))
                    start(attention(h))
                tk["last"] = tp

            projects((Hh, Hl), lambda k: h_toks[k], 24, evac)
            h_last = tk["last"]
            tick()
            o_last = wo(o_toks, MOD[:, 1, 16:24], lambda: [t_mod[1, 4], t_mod[1, 5]], 6)
            mix_done = [PE.now(), AC.now(), DV.now(), PO.now()]
        flush()
        if debug == 2:
            SP.dma(lambda e: e.dma_start(out, X[:]), cnt("out"), ssq["last"])
            SP.wait((counters["out"][0], counters["out"][1]))
            return
        h_toks = norm([h_last], SC[:, 3, :], MOD[:, 1, 24:32], (t_mod[1, "A", 1], t_mod[1, 6], t_mod[1, 7]))
        h_last, o_last = mlp(1, h_toks)
        if debug == 3:
            SP.dma(lambda e: e.dma_start(out, X[:]), cnt("out"), ssq["last"])
            SP.wait((counters["out"][0], counters["out"][1]))
            return
        h_toks = norm([h_last], g="fin")

        with ExitStack() as ph:
            SEL = sb("SEL", [P, 1152], c=ph)
            MKP = sb("MK", [P, 1280], c=ph)
            MK = [MKP[:, 64 * i * (i + 1):64 * (i + 1) * (i + 2)] for i in range(4)]
            cT, ctok = sb("cT", [P, T], c=ph), sb("ctok", [P, 4, 128], c=ph)
            K, Q, Bc, SH, vT = (sb(n, [P, 4, T], c=ph) for n in ("K2", "Q2", "B2", "SH", "vT2"))
            FB = sb("FB", [P, 6, T], c=ph)
            iwt, m8 = sb("iwt", [P, 4, 8], c=ph), sb("m8", [P, 3, 8], c=ph)
            dec = sb("dec2", [P, 4, 8], c=ph)
            lb2 = sb("lb2", [P, 6, 4], c=ph)
            st = sb("st2", [P, 8, 4], c=ph)
            wuk, wuv = sb("wuk", [P, 4, 128], c=ph), sb("wuv", [P, 4, 128], c=ph)
            relb = sb("relb", [32, 4], c=ph)
            scr = nc.dram_tensor("scr", (4, 128, 640), F, kind="Internal").ap()
            for q in (SP, AC, DV, PO, PE):
                q.wait(mix_done)
            SL = {1: (0, 256), 2: (256, 384), 3: (640, 512)}
            sel = {i: SEL[:, o:o + n] for i, (o, n) in SL.items()}
            t_uk = SP.dma(lambda e: e.dma_start(wuk[:], D["w_uk"].rearrange("p (h r) -> p h r", h=4)), cnt("wuk"))
            t_uv = SP.dma(lambda e: e.dma_start(wuv[:], D["w_uv"].rearrange("p (h r) -> p h r", h=4)), cnt("wuv"))
            t_rel = SP.dma(lambda e: e.dma_start(relb[:], D["rel"]), cnt("rel"))
            ada = ADA[:].rearrange("p a t -> p (a t)")
            hot = ada[0:32, 0:640]
            t_hot = SP.dma(lambda e: e.dma_start(hot, D["hot"]), cnt("hot"), mix_done)

            rb = SH[0:32, 0, :].rearrange("p (h m) -> p h m", h=4)
            t_rb = DV(lambda e: e.tensor_copy(rb, relb[:].unsqueeze(2).to_broadcast([32, 4, 128])), t_rel)
            t_scr = []
            for h in range(4):
                for o, n in ((0, 512), (512, 128)):
                    bi, bank, w = tb.take()
                    tp = PE(lambda e: e.matmul(bank[:, 0:n], rb[:, h, :], hot[:, o:o + n], start=True, stop=True),
                            t_rb, t_hot, w)
                    i1, a1, w1 = tmp.take()
                    a = AC(lambda e: e.activation(a1[:, 0:n], bank[:, 0:n], ACT.Copy), tp, w1)
                    tb.give(bi, a)
                    t = SP.dma(lambda e: e.dma_start(scr[h][:, o:o + n], a1[:, 0:n]), cnt(f"scr{h}{o}"), a)
                    tmp.give(i1, t)
                    t_scr.append(t)

            l0, l1 = V("lb", 0, 4), V("lb", 4, 4)
            t = DV(lambda e: e.tensor_tensor(lb2[:, 0, :], l0, l1, ALU.max))
            ta = DV(lambda e: e.tensor_tensor(lb2[:, 1, :], l0, lb2[:, 0, :], ALU.subtract), t)
            tx = DV(lambda e: e.tensor_tensor(lb2[:, 2, :], l1, lb2[:, 0, :], ALU.subtract), t)
            t = AC(lambda e: e.activation(lb2[:, 1:3, :], lb2[:, 1:3, :], ACT.Exp), ta, tx)
            t = DV(lambda e: e.tensor_tensor(lb2[:, 3, :], lb2[:, 1, :], lb2[:, 2, :], ALU.add), t)
            t = DV(lambda e: e.reciprocal(lb2[:, 3, :], lb2[:, 3, :]), t)
            t = DV(lambda e: e.tensor_tensor(lb2[:, 4, :], lb2[:, 1, :], lb2[:, 3, :], ALU.mult), t)
            t_lb = DV(lambda e: e.tensor_scalar(lb2[:, 5, :], lb2[:, 4, :], -1.0, 1.0, ALU.mult, ALU.add), t)
            lb, oml = lb2[:, 4, :], lb2[:, 5, :]

            tk = {}
            O = PS[:, 7, :]
            gs = Slots([PS[:, i, :] for i in (4, 5, 6)])
            FR = Slots([FB[:, i, :] for i in range(2, 6)])
            late = [FB[:, 0, :], FB[:, 1, :]]
            wk = Slots([])
            S = ada[:, 0:896].rearrange("p (n v) -> p n v", v=128)
            ik = FB[:, 0, :]
            SCALE = 128.0 ** -0.5
            IQ = vT
            idx_done = []
            acc = {}
            o_toks = [None] * 8
            t_sh = PO(lambda e: e.memset(SH[:], 0.0), t_rb, t_scr)
            t_mk = {0: DV(lambda e: e.tensor_scalar(MK[0], C("adm"), NEG, None, ALU.max))}
            todo = [(r, i) for r in range(16) for i in (1, 2, 3)]

            def top(n):
                for _ in range(min(n, len(todo))):
                    r, i = todo.pop(0)
                    t = DV(lambda e: e.max(m8[:, i - 1, :], sel[i]), acc[i])
                    acc[i] = DV(lambda e: e.match_replace(sel[i], m8[:, i - 1, :], sel[i], TAKEN), t)
                    if r == 15:
                        t = DV(lambda e: e.tensor_scalar(MK[i], sel[i], -3.3e38, -1.0, ALU.is_le, ALU.add), acc[i])
                        t_mk[i] = DV(lambda e: e.tensor_scalar(MK[i], MK[i], -NEG, None, ALU.mult), t)

            def indexer(a1, a2, t_ik):
                yield
                bi, bank, w = tb.take()
                for i in range(4):
                    tp = PE(lambda e: e.transpose(bank[:, i * 8:(i + 1) * 8], FB[64:72, 1, i * 128:(i + 1) * 128],
                                                  ident[64:72, 64:72]), a2, w, inc=i == 3)
                t_iw = DV(lambda e: e.tensor_scalar(iwt[:].rearrange("p a b -> p (a b)"), bank[:, 0:32], 8.0 ** -0.5, None,
                                                    ALU.mult), tp)
                tb.give(bi, t_iw)
                for i, e8 in ((i, e8) for i in (1, 2, 3) for e8 in range(8)):
                    L = 128 * (i + 1)
                    r = slice(64 * (e8 % 2), 64 * (e8 % 2) + 64)
                    gi, g, w = gs.take()
                    tp = PE(lambda e: e.matmul(g[:, 0:L], IQ[r, e8 // 2, i * 128:(i + 1) * 128], ik[r, 0:L],
                                               start=True, stop=True), [tk["iq", j] for j in range(4)], a1, t_ik, w)
                    i1, b1, w1 = tmp.take()
                    a = AC(lambda e: e.activation(b1[:, 0:L], g[:, 0:L], ACT.Relu, scale=0.125), tp, w1)
                    gs.give(gi, a)
                    if e8 == 0:
                        t = DV(lambda e: e.tensor_scalar(sel[i], b1[:, 0:L], iwt[:, i, 0:1], 0.0, ALU.mult, ALU.add),
                               a, t_iw)
                    else:
                        t = DV(lambda e: e.scalar_tensor_tensor(sel[i], b1[:, 0:L], iwt[:, i, e8:e8 + 1], sel[i],
                                                                ALU.mult, ALU.add), a, t)
                    tmp.give(i1, t)
                    if e8 == 7:
                        acc[i] = DV(lambda e: e.tensor_tensor(sel[i][:, L - 128:L], sel[i][:, L - 128:L], C("adm"),
                                                              ALU.add), t)
                    if e8 in (3, 7) and (i, e8) != (3, 7):
                        yield
                idx_done.append(tp)
                for x, t_ in zip(late, (tp, t_iw)):
                    FR.bufs.append(x)
                    FR.give(len(FR.bufs) - 1, t_, t_ik, tp)

            def latent(bi, bank, tp):
                i1, b1, w1 = tmp.take()
                i2, b2, w2 = tmp.take()
                c = AC(lambda e: e.activation(b2, bank, ACT.Copy), tp, w2)
                pj.give(bi, c)
                a = AC(lambda e: e.activation(b1, b2, ACT.Square), c, w1)
                yield
                bi, bank, w = tb.take()
                m = PE(lambda e: e.matmul(bank, ones[:], b1, start=True, stop=True), a, w)
                tr = rstd_of(bank, m, b1, 128, epsb[:, 0:1])
                tb.give(bi, tr)
                tk["cT"] = DV(lambda e: e.scalar_tensor_tensor(cT[:], b2, V("kv_g"), b1, ALU.mult, ALU.mult), tr)
                tmp.give(i1, tk["cT"])
                tmp.give(i2, tk["cT"])
                yield
                bi, bank, w = tb.take()
                tp = turned(bank, cT[:], tk["cT"], w)
                tk["ct"] = AC(lambda e: e.activation(ctok[:].rearrange("p a r -> p (a r)"), bank, ACT.Copy), tp)
                tb.give(bi, tk["ct"])

            def recurrence(h):
                Bh, Kh, Qh = Bc[:, h, :], K[:, h, :], Q[:, h, :]
                kq = [tk["k", h], tk["q", h]]
                F_ = {}

                def ready_level(lv):
                    half = LEVELS[lv]
                    two = lambda x: x.rearrange("p (n a c) -> p n a c", a=2, c=half)
                    full = lambda x: x.rearrange("p (n c) -> p n c", c=2 * half)
                    fi, f, w = FR.take()
                    ref = full(Bh)[:, :, half - 1:half].to_broadcast([P, 256 // half, 2 * half])
                    d = PO(lambda e: e.tensor_tensor(full(f), full(Bh), ref, ALU.subtract), tk["b", h], w)
                    e1 = AC(lambda e: e.activation(two(f)[:, :, 0], two(f)[:, :, 0], ACT.Exp, scale=-1.0), d)
                    e2 = AC(lambda e: e.activation(two(f)[:, :, 1], two(f)[:, :, 1], ACT.Exp), d)
                    x1 = PO(lambda e: e.tensor_tensor(two(f)[:, :, 0], two(f)[:, :, 0], two(Kh)[:, :, 0], ALU.mult), e1, kq)
                    x2 = DV(lambda e: e.tensor_tensor(two(f)[:, :, 1], two(f)[:, :, 1], two(Qh)[:, :, 1], ALU.mult), e2, kq)
                    F_[lv] = (fi, f, [x1, x2])

                def level(lv):
                    if lv < 6:
                        fi, left, have = F_[lv]
                        right = left
                    else:
                        left, right, have = Kh, Qh, kq
                    gi, g, w = gs.take()
                    for t in range(4):
                        ts = slice(t * 128, (t + 1) * 128)
                        tp = PE(lambda e: e.matmul(g[:, ts], left[:, ts], right[:, ts], start=True, stop=True),
                                have, w, inc=t == 3)
                    o = CON["lev"][0] + lv * 128
                    mask = con[:, o:o + 128].bitcast(U32).unsqueeze(1).to_broadcast([P, 4, 128])
                    tk["sh", h] = DV(lambda e: e.copy_predicated(four(SH[:, h, :]), mask, four(g)), tp,
                                  tk.get(("sh", h), t_sh))
                    gs.give(gi, tk["sh", h])
                    if lv < 6:
                        FR.give(fi, tp)
                    return tp

                yield
                ready_level(0)
                ready_level(1)
                yield
                level(0)
                level(1)
                ready_level(2)
                ready_level(3)
                yield
                level(2)
                level(3)
                ready_level(4)
                ready_level(5)
                yield
                level(4)
                level(5)
                dg = level(6)
                i1, b1, w1 = tmp.take()
                b3 = Bh.rearrange("p (n c) -> p n c", c=64)
                t = DV(lambda e: e.tensor_tensor(b1.rearrange("p (n c) -> p n c", c=64), b3,
                                                 b3[:, :, 63:64].to_broadcast([P, 8, 64]), ALU.subtract), tk["b", h], w1)
                a = AC(lambda e: e.activation(b1, b1, ACT.Exp, scale=-1.0), t)
                a0 = AC(lambda e: e.activation(Bh, Bh, ACT.Exp), t)
                t = DV(lambda e: e.tensor_tensor(b1, b1, Kh, ALU.mult), a)
                d = DV(lambda e: e.tensor_copy(dec[:, h, :], Bh.rearrange("p (n c) -> p n c", c=64)[:, :, 63]), a0)
                qx = DV(lambda e: e.tensor_tensor(Qh, Bh, Qh, ALU.mult), a0, dg)
                tk["free", h] = [dg, d, qx, t]
                yield
                bi, bank, w = tb.take()
                tp = turned(bank, b1, t, w)
                i2, b2, w2 = tmp.take()
                tmp.give(i1, tp)
                ks = AC(lambda e: e.activation(b2, bank, ACT.Copy), tp, w2)
                tb.give(bi, ks)
                yield
                res = {}
                vh = four(vT[:, h, :])
                steps = state_and_values(lambda t: SH[:, h, t * 128:(t + 1) * 128], tk["sh", h], four(b2), ks, vh,
                                         tk["v", h], Qh, qx, dec[:, h, :], d, S, [tk.get("S"), t_hotdone], gs, [O],
                                         tk.get("O"), 1, res)
                next(steps)
                yield
                next(steps, 0)
                tp = res["tp"]
                tk["S"] = tp
                tmp.give(i2, tp)
                i3, on, w3 = tmp.take()
                i4, sq, w4 = tmp.take()
                c = AC(lambda e: e.activation(on, O, ACT.Copy), tp, w3)
                tk["O"] = c
                a = AC(lambda e: e.activation(sq, on, ACT.Square), c, w4)
                for x in (SH[:, h, :], vT[:, h, :]):
                    wk.bufs.append(x)
                    wk.give(len(wk.bufs) - 1, tp)
                yield
                bi, bank, w = tb.take()
                m = PE(lambda e: e.matmul(bank, ones[:], sq, start=True, stop=True), a, w)
                tr = rstd_of(bank, m, sq, 128, epsb[:, 0:1])
                tb.give(bi, tr)
                tk["ob", h] = DV(lambda e: e.scalar_tensor_tensor(Qh, on, V("hg_g", h), sq, ALU.mult, ALU.mult), tr, tp)
                tmp.give(i3, tk["ob", h])
                tmp.give(i4, tk["ob", h])

            def queries(h, bi, bank, tp):
                i1, qa, w1 = tmp.take()
                a = AC(lambda e: e.activation(qa, bank, ACT.Copy), tp, w1)
                pj.give(bi, a)
                yield
                bi, bank, w = tb.take()
                tp = PE(lambda e: e.matmul(bank, wuk[:, h, :], qa, start=True, stop=True), a, t_uk, w)
                tmp.give(i1, tp)
                tk["ql", h] = AC(lambda e: e.activation(K[:, h, :], bank, ACT.Copy), tp, tk["free", h])
                tb.give(bi, tk["ql", h])

            TB = {}

            def attend(h):
                def logits(i):
                    L = 128 * (i + 1)
                    sl = st[:, (4 * h + i) % 8, :]
                    gi, g, w = gs.take()
                    tp = PE(lambda e: e.matmul(g[:, 0:L], K[:, h, i * 128:(i + 1) * 128], cT[:, 0:L], start=True, stop=True),
                            tk["ql", h], tk["cT"], w)
                    pi, p, w = wk.take()
                    t = DV(lambda e: e.scalar_tensor_tensor(p[:, 0:L], g[:, 0:L], SCALE, TB[h][0][:, 384 - 128 * i:512],
                                                            ALU.mult, ALU.add), tp, w, TB[h][1])
                    gs.give(gi, t)
                    t = DV(lambda e: e.tensor_tensor(p[:, 0:L], p[:, 0:L], MK[i], ALU.add), t, t_mk[i])
                    t = DV(lambda e: e.reduce_max(sl[:, 0:1], p[:, 0:L], axis=AX.X, negate=True), t)
                    t = AC(lambda e: e.activation(p[:, 0:L], p[:, 0:L], ACT.Exp, bias=sl[:, 0:1], accum_out=sl[:, 1:2]), t)
                    t2 = DV(lambda e: e.reciprocal(sl[:, 2:3], sl[:, 1:2]), t)
                    t = DV(lambda e: e.tensor_scalar(p[:, 0:L], p[:, 0:L], sl[:, 2:3], None, ALU.mult), t2)
                    tk["p", i, h] = (pi, p, t)

                def turn(i):
                    pi, p, t = tk.pop(("p", i, h))
                    bi, bank, w = tb.take()
                    tp = turned(bank, p, t, w, i + 1)
                    wk.give(pi, tp)
                    ai, aT, w = wk.take()
                    a = AC(lambda e: e.activation(aT[:, 0:128 * (i + 1)], bank[:, 0:128 * (i + 1)], ACT.Copy), tp, w)
                    tb.give(bi, a)
                    tk["T", i, h] = (ai, aT, a)

                def weigh(i):
                    ai, aT, a = tk.pop(("T", i, h))
                    for s in range(i + 1):
                        tp = PE(lambda e: e.matmul(O[:, i * 128:(i + 1) * 128], ctok[:, s, :],
                                                   aT[:, s * 128:(s + 1) * 128], start=s == 0, stop=s == i),
                                a, tk["ct"], tk["O"], inc=s == i)
                    wk.give(ai, tp)
                    return tp

                yield
                logits(3)
                logits(2)
                yield
                turn(3)
                logits(1)
                logits(0)
                turn(2)
                yield
                weigh(3)
                turn(1)
                turn(0)
                weigh(2)
                yield
                weigh(1)
                tp = weigh(0)
                i1, ol, w1 = wk.take()
                a = AC(lambda e: e.activation(ol, O, ACT.Copy), tp, w1)
                tk["O"] = a
                yield
                bi, bank, w = tb.take()
                tp = PE(lambda e: e.matmul(bank, wuv[:, h, :], ol, start=True, stop=True), a, t_uv, w)
                wk.give(i1, tp)
                t = DV(lambda e: e.tensor_tensor(Bc[:, h, :], bank, Bc[:, h, :], ALU.mult), tp, tk["ga", h])
                tb.give(bi, t)
                o_toks[h] = split_out(Bc[:, h, :], Oh[:, h, :], Ol[:, h, :], t, o_last)

            kinds = [("iq", j) for j in range(4)] + [("ik", 0), ("c", 0)]
            for h in range(4):
                kinds += [("f", h), ("q", h), ("i", h)]
            kinds += [("qa", h) for h in range(4)]
            kinds += [("gb", 0), ("gb", 1), ("ga", 0), ("ga", 1), ("gb", 2), ("ga", 2), ("gb", 3), ("ga", 3)]
            t_hotdone = t_hot

            def evac(n, bi, bank, tp):
                kind, h = kinds[n]
                tk["last"] = tp
                if kind == "iq":
                    tk["iq", h] = AC(lambda e: e.activation(IQ[:, h, :], bank, ACT.Copy), tp)
                    pj.give(bi, tk["iq", h])
                elif kind == "ik":
                    a1 = AC(lambda e: e.activation(ik[0:64, :], bank[0:64, :], ACT.Copy), tp)
                    a2 = AC(lambda e: e.activation(FB[64:72, 1, :], bank[64:72, :], ACT.Copy), tp)
                    pj.give(bi, a2)
                    t_ik = SP.dma(lambda e: e.dma_start(ik[64:128, :], ik[0:64, :]), cnt("ik"), a1)
                    start(indexer(a1, a2, t_ik))
                elif kind == "c":
                    start(latent(bi, bank, tp))
                elif kind == "f":
                    i1, s1, w1 = tmp.take()
                    a = sigmoid(s1, bank, tp, w1)
                    pj.give(bi, a)
                    x = DV(lambda e: e.tensor_scalar(s1, s1, oml[:, h:h + 1], lb[:, h:h + 1], ALU.mult, ALU.add), a, t_lb)
                    tk["k", h] = DV(lambda e: e.tensor_scalar(K[:, h, :], s1, -1.0, 1.0, ALU.mult, ALU.add), x)
                    i2, s2, w2 = tmp.take()
                    a = AC(lambda e: e.activation(s2, s1, ACT.Ln), x, w2)
                    tmp.give(i1, a, tk["k", h])
                    tk["b", h] = DV(lambda e: e.tensor_tensor_scan(Bc[:, h, :], C("scan"), s2, 0.0, ALU.mult, ALU.add), a)
                    tmp.give(i2, tk["b", h])
                elif kind == "q":
                    start(query(h, bi, bank, tp))
                elif kind == "i":
                    start(values(four(vT[:, h, :]), bi, bank, tp, tk, ("v", h), idx_done))
                    start(recurrence(h))
                elif kind == "qa":
                    start(queries(h, bi, bank, tp))
                elif kind == "ga":
                    i1, s1, w1 = tmp.take()
                    a = sigmoid(s1, bank, tp, w1)
                    tk["ga", h] = DV(lambda e: e.tensor_tensor(Bc[:, h, :], bank, s1, ALU.mult), a, tk["free", h])
                    pj.give(bi, tk["ga", h])
                    tmp.give(i1, tk["ga", h])
                else:
                    i3, sg, w3 = tmp.take()
                    a = sigmoid(sg, bank, tp, w3)
                    t = DV(lambda e: e.tensor_tensor(sg, bank, sg, ALU.mult), a)
                    pj.give(bi, t)
                    start(gate_b(h, i3, sg, t))
                if n == 22:
                    wk.bufs += [FB[:, 4, :], FB[:, 5, :]]
                    for i in (-2, -1):
                        wk.give(len(wk.bufs) + i, *[t_ for _, w in FR.free for t_ in w])
                    for h_ in range(4):
                        ap = scr[h_]
                        skew = bass.AP(tensor=ap.tensor, offset=ap.offset + 127, ap=[[639, 128], [1, 512]])
                        t_ = SP.dma(lambda e: e.dma_start(FB[:, h_, :], skew), cnt(f"tb{h_}"),
                                    [t2 for _, w in FR.free for t2 in w], t_scr)
                        TB[h_] = (FB[:, h_, :], t_)
                if n in (23, 25, 27, 29):
                    start(attend((n - 23) // 2))

            def query(h, bi, bank, tp):
                i1, s1, w1 = tmp.take()
                a = sigmoid(s1, bank, tp, w1)
                tk["q", h] = DV(lambda e: e.tensor_tensor(Q[:, h, :], bank, s1, ALU.mult), a)
                pj.give(bi, tk["q", h])
                tmp.give(i1, tk["q", h])
                return
                yield

            def gate_b(h, i3, sg, t):
                while ("ob", h) not in tk:
                    yield
                t = DV(lambda e: e.tensor_tensor(sg, sg, Q[:, h, :], ALU.mult), t, tk["ob", h])
                o_toks[4 + h] = split_out(sg, Oh[:, 4 + h, :], Ol[:, 4 + h, :], t, o_last)
                tmp.give(i3, *o_toks[4 + h])

            def side():
                if 3 in acc:
                    top(4)

            projects((Hh, Hl), lambda k: h_toks[k], 30, evac, ms={4: 72}, side=side)
            tick()
            sums = {}

            def evac_out(j, bi, bank, tp):
                t = DV(lambda e: e.scalar_tensor_tensor(X[:, j, :], X[:, j, :], ALPHA, bank, ALU.mult, ALU.add), tp)
                pj.give(bi, t)
                sums["x"] = t
                if j == 0:
                    sums["s"] = PO(lambda e: e.tensor_copy(SSQ[:], X[:, 0, :]), t, ssq["free"])
                elif j < 7:
                    sums["s"] = PO(lambda e: e.tensor_tensor(SSQ[:], SSQ[:], X[:, j, :], ALU.add), t, sums["s"])

            projects((Oh, Ol), lambda k: o_toks[k], 8, evac_out, ks=5, order=(4, 5, 6, 7, 0, 1, 2, 3))

            bi, bank, w = tb.take()
            PE(lambda e: e.matmul(bank, ones[:], SSQ[:], start=True, stop=False), sums["s"], w, inc=False)
            tp = PE(lambda e: e.matmul(bank, ones[:], X[:, 7, :], start=False, stop=True), sums["x"])
            b2i, bank2, w2 = tb.take()
            for j in range(8):
                t = DV(lambda e: e.scalar_tensor_tensor(X[:, j, :], bank, -1.0 / 1024, X[:, j, :], ALU.mult, ALU.add), tp)
                i1, sq, w1 = tmp.take()
                a = AC(lambda e: e.activation(sq, X[:, j, :], ACT.Square), t, w1)
                m = PE(lambda e: e.matmul(bank2, ones[:], sq, start=j == 0, stop=j == 7), a, w2)
                tmp.give(i1, m)
            tr = rstd_of(bank2, m, RS[:], 1024, epsb[:, 1:2], ssq["free"])
            for j in range(8):
                t = DV(lambda e: e.scalar_tensor_tensor(X[:, j, :], X[:, j, :], V("ln_g", j), RS[:], ALU.mult, ALU.mult), tr)
                t = AC(lambda e: e.activation(X[:, j, :], X[:, j, :], ACT.Identity, bias=V("ln_b", j)), t)
                SP.dma(lambda e: e.dma_start(out[:, j, :], X[:, j, :]), cnt("out"), t)
        SP.wait((counters["out"][0], counters["out"][1]))


def shape_constants():
    con = np.zeros((P, NCON), np.float32)

    def put(name, a):
        o, n = CON[name]
        con[:, o:o + n] = a

    s, t = np.arange(P)[:, None], np.arange(P)[None, :]
    put("ident", (s == t))
    put("tri", (s // 64 == t // 64) & (s <= t))
    put("scan", np.broadcast_to((np.arange(T) % 64 != 0).astype(np.float32), (P, T)))
    lev = [(s // (2 * h) == t // (2 * h)) & (s // h % 2 == 0) & (t // h % 2 == 1) for h in LEVELS] + [s == t]
    put("lev", np.concatenate(lev, axis=1))
    rot = np.zeros((P, P), np.float32)
    for b in (0, 64):
        for i in range(8):
            rot[b + 8 + i, b + i] = -1.0
            rot[b + i, b + 8 + i] = 1.0
    put("rot", rot)
    put("adm", np.where(t // 64 <= s // 64, 0.0, FILL))
    put("cau", np.where(t <= s, 0.0, NEG))
    inv = (np.float32(500000.0) ** (-np.arange(0, 16, 2, dtype=np.float32) / np.float32(16))).astype(np.float32)
    p = np.arange(P) % 64
    put("freq", np.where(p < 16, inv[p % 8], 0.0).astype(np.float32)[:, None])
    rel = np.arange(640) - 511
    n = np.abs(rel)
    nf = np.maximum(n, 1).astype(np.float32)
    large = 8 + (np.log(nf / np.float32(8)) / np.float32(math.log(32.0)) * np.float32(8)).astype(np.int32)
    buck = np.where(rel > 0, 16, 0) + np.where(n < 8, n, np.minimum(large, 15))
    hot = (np.arange(32)[:, None] == buck[None, :]).astype(np.float32)
    return con, hot


def tiles(w, cols=128):
    w = np.ascontiguousarray(w)
    n = w.shape[1] // cols
    return np.ascontiguousarray(w.reshape(8, P, n, cols).transpose(2, 1, 0, 3)).reshape(n, P, 8 * cols)


def layout(i):
    col = lambda v: np.ascontiguousarray(v).reshape(-1, P).T
    a = {k: np.asarray(v) for k, v in i.items()}
    con, hot = shape_constants()
    parts = [a["c"], a["norm_g"][0, 0], a["norm_g"][0, 1], a["norm_g"][1, 0], a["norm_g"][1, 1], a["final_g"],
             a["ada_b"], a["gla_b_a"], a["gla_b_r"], a["gla_norm_g"], a["diff_subln_g"], a["kv_norm_g_2"],
             a["hgrn_norm_g_2"], a["lb_logits_2"], a["ln_g_2"], a["ln_b_2"]]
    d = {"con": con, "hot": hot, "vec": np.ascontiguousarray(np.concatenate([col(v) for v in parts], axis=1))}
    d["xT"] = np.ascontiguousarray(a["x"][0].T)
    d["pos"] = np.ascontiguousarray(a["positions"])
    d["ada"] = np.ascontiguousarray(a["ada_w"].reshape(2, 4, 2, P, 12, T).transpose(0, 4, 1, 3, 2, 5)).reshape(2, 12, 4, P, 2 * T)
    g = a["gla_w_in"][0]
    d["gla_in"] = tiles(g[:, :3072])
    d["w_a"] = tiles(g[:, 3072:], 16)[0]
    d["w_a2"] = np.ascontiguousarray(a["gla_w_a2"][0])
    d["gla_wo"] = tiles(a["gla_w_o"][0])
    for l in range(2):
        d[f"w1_{l}"] = tiles(a["mlp_w1"][l])
        d[f"w2_{l}"] = np.concatenate([tiles(a["mlp_w2"][l][r * 1024:(r + 1) * 1024]) for r in range(4)])
    d["diff_in"] = tiles(a["diff_w_in"][0])
    d["diff_wo"] = tiles(a["diff_w_o"][0])
    d["lam"] = np.ascontiguousarray(a["diff_lambda"][0].reshape(1, 256))
    w = a["w_in_2"][0]
    d["in_q"] = tiles(w[:, 0:512])
    d["in_c"] = tiles(w[:, 512:640])
    d["in_iq"] = tiles(w[:, 640:1152])
    d["in_ik"] = tiles(w[:, 1152:1224], 72)[0]
    d["in_ag"] = tiles(w[:, 1224:1736])
    d["in_b"] = tiles(w[:, 1736:3784])
    d["w_uk"] = np.ascontiguousarray(a["w_uk_2"][0].transpose(1, 0, 2)).reshape(P, 512)
    d["w_uv"] = np.ascontiguousarray(a["w_uv_2"][0].transpose(1, 0, 2)).reshape(P, 512)
    d["rel"] = np.ascontiguousarray(a["rel_bias_2"])
    d["wo_2"] = tiles(a["w_o_2"][0])
    return d


def kernel(**inputs):
    import concourse.bacc as bacc
    from concourse.bass_utils import run_bass_kernel_spmd

    nc = bacc.Bacc("TRN2", target_bir_lowering=False, num_devices=1, dynamic_dma_scratch_size=2048)
    arrays = layout(inputs)
    D = {k: nc.dram_tensor(k, v.shape, mybir.dt.from_np(v.dtype), kind="ExternalInput").ap() for k, v in arrays.items()}
    out = nc.dram_tensor("yT", (P, 8, T), F, kind="ExternalOutput").ap()
    build(nc, D, out)
    r = run_bass_kernel_spmd(nc, [arrays], core_ids=[0])
    y = r.results[0]["yT"]
    return np.ascontiguousarray(y.transpose(2, 1, 0)).reshape(1, T, 1024)
```
